# Optimizing a Trainium2 kernel written in Bass

```python
import math
import jax, jax.numpy as jnp
from jax import lax
import numpy as np

D_MODEL = 1024
BATCH = 1
SEQ = 256
DEPTH = 1
DEC_BATCH = 8
DEC_SEQ = 8
PAST_LEN = 2048
PAGE_SIZE = 128

N_META = 16
D_CONV = D_MODEL
CONV_K = 31
D_INNER = 2 * D_MODEL
N_HEADS = 4
HEAD_DIM = D_INNER // N_HEADS
QKV_BLOCK = 4
MCONV_K = 4
CHUNK = 64
N_EXPERTS = 64
TOP_K = 8
N_GROUPS = 8
TOPK_GROUPS = 4
D_EXPERT = D_MODEL // 4
D_SHARED = D_EXPERT
ROUTE_SCALE = 2.5
EXPERT_BLOCK = 128
ALPHA = (2 * DEPTH) ** 0.25
BETA = (8 * DEPTH) ** -0.25
LN_EPS = 1e-5
IN_SPLITS = [D_CONV, 2 * D_CONV, 2 * D_CONV + D_INNER, 2 * D_CONV + 2 * D_INNER, 2 * D_CONV + 2 * D_INNER + D_MODEL]
N_IN = 2 * D_CONV + 2 * D_INNER + 2 * D_MODEL

kernel_name = 'conformer_mlstm_gated_moe_deepnorm_step'

def layer_norm(x, g, b=None):
    xf = x.astype(jnp.float32)
    mu = jnp.mean(xf, axis=-1, keepdims=True)
    var = jnp.mean(jnp.square(xf - mu), axis=-1, keepdims=True)
    y = (xf - mu) * lax.rsqrt(var + LN_EPS) * g.astype(jnp.float32)
    if b is not None:
        y = y + b.astype(jnp.float32)
    return y.astype(x.dtype)

def causal_dwconv(u, buf, w, b):
    full = jnp.concatenate([buf.astype(u.dtype), u], axis=1)
    out = lax.conv_general_dilated(full, w[:, None, :].astype(u.dtype), window_strides=(1,), padding='VALID',
                                   dimension_numbers=('NWC', 'WIO', 'NWC'), feature_group_count=u.shape[-1])
    return out + b.astype(u.dtype), full[:, -(w.shape[0] - 1):]

def headwise(x, w):
    B, L, _ = x.shape
    xb = x.reshape(B, L, w.shape[0], w.shape[1])
    return jnp.einsum('blni,nio->blno', xb, w.astype(x.dtype)).reshape(B, L, -1)

def mlstm_chunk(state, inp):
    C0, n0, m0 = state
    q, k, v, ig, lf = inp
    L = q.shape[2]
    b = jnp.cumsum(lf, axis=-1)
    causal = jnp.tril(jnp.ones((L, L), dtype=bool))
    log_w = jnp.where(causal, b[..., :, None] - b[..., None, :] + ig[..., None, :], -jnp.inf)
    log_s = b + m0[..., None]
    m = jnp.maximum(log_s, jnp.max(log_w, axis=-1))
    w = jnp.exp(log_w - m[..., None])
    s = jnp.exp(log_s - m)
    qk = jnp.einsum('bhtd,bhsd->bhts', q, k) * w
    num = s[..., None] * jnp.einsum('bhtd,bhde->bhte', q, C0) + jnp.einsum('bhts,bhse->bhte', qk, v)
    den = s * jnp.einsum('bhtd,bhd->bht', q, n0) + jnp.sum(qk, axis=-1)
    h = num / jnp.maximum(jnp.abs(den), jnp.exp(-m))[..., None]
    m_end = m[..., -1]
    w_end = jnp.exp(b[..., -1:] - b + ig - m_end[..., None])
    s_end = jnp.exp(b[..., -1] + m0 - m_end)
    C1 = s_end[..., None, None] * C0 + jnp.einsum('bhsd,bhse->bhde', k * w_end[..., None], v)
    n1 = s_end[..., None] * n0 + jnp.einsum('bhs,bhsd->bhd', w_end, k)
    return (C1, n1, m_end), h

def mlstm_sequence(q, k, v, ig, lf, state, lead, chunk):
    parts = []
    if lead > 0:
        state, h0 = mlstm_chunk(state, (q[:, :, :lead], k[:, :, :lead], v[:, :, :lead], ig[..., :lead], lf[..., :lead]))
        parts.append(h0)
    rest = q.shape[2] - lead
    nc = rest // chunk

    def to_chunks(a):
        a = a[:, :, lead:]
        a = a.reshape(a.shape[:2] + (nc, chunk) + a.shape[3:])
        return jnp.moveaxis(a, 2, 0)

    state, hr = lax.scan(mlstm_chunk, state, tuple(to_chunks(a) for a in (q, k, v, ig, lf)))
    hr = jnp.moveaxis(hr, 0, 2).reshape(q.shape[:2] + (rest, v.shape[-1]))
    parts.append(hr)
    return state, jnp.concatenate(parts, axis=2)

def mix_sublayer(h, conv_buf, mconv_buf, C0, n0, m0, lead, chunk,
                 w_in, conv_w, conv_b, conv_ln_g, conv_ln_b, w_conv_out, mconv_w, mconv_b,
                 w_q, w_k, w_v, w_if, b_if, mh_ln_g, skip, w_m_down, w_o):
    B, L, _ = h.shape
    f32 = jnp.float32
    proj = h @ w_in.astype(h.dtype)
    glu_a, glu_b, xm, og, ga, gb = jnp.split(proj, IN_SPLITS, axis=-1)
    u = glu_a * jax.nn.sigmoid(glu_b)
    ca, conv_buf_new = causal_dwconv(u, conv_buf, conv_w, conv_b)
    ya = jax.nn.silu(layer_norm(ca, conv_ln_g, conv_ln_b)) @ w_conv_out.astype(h.dtype)
    cm, mconv_buf_new = causal_dwconv(xm, mconv_buf, mconv_w, mconv_b)
    cm = jax.nn.silu(cm)
    q = headwise(cm, w_q)
    k = headwise(cm, w_k)
    v = headwise(xm, w_v)
    gates = jnp.concatenate([q, k, v], axis=-1).astype(f32) @ w_if.astype(f32) + b_if.astype(f32)
    ig = jnp.transpose(gates[..., :N_HEADS], (0, 2, 1))
    lf = jnp.transpose(jax.nn.log_sigmoid(gates[..., N_HEADS:]), (0, 2, 1))
    to_heads = lambda a: jnp.transpose(a.astype(f32).reshape(B, L, N_HEADS, HEAD_DIM), (0, 2, 1, 3))
    qh = to_heads(q)
    kh = to_heads(k) * (HEAD_DIM ** -0.5)
    vh = to_heads(v)
    state0 = (C0.astype(f32), n0.astype(f32), m0.astype(f32))
    (C1, n1, m1), hh = mlstm_sequence(qh, kh, vh, ig, lf, state0, lead, chunk)
    mu = jnp.mean(hh, axis=-1, keepdims=True)
    var = jnp.mean(jnp.square(hh - mu), axis=-1, keepdims=True)
    hh = (hh - mu) * lax.rsqrt(var + LN_EPS)
    hh = jnp.transpose(hh, (0, 2, 1, 3)).reshape(B, L, D_INNER) * mh_ln_g.astype(f32)
    hb = (hh.astype(h.dtype) + skip.astype(h.dtype) * cm) * jax.nn.sigmoid(og)
    yb = hb @ w_m_down.astype(h.dtype)
    merged = jax.nn.sigmoid(ga) * ya + jax.nn.sigmoid(gb) * yb
    return merged @ w_o.astype(h.dtype), conv_buf_new, mconv_buf_new, C1, n1, m1

def swiglu(x, w1, w3, w2):
    return (jax.nn.silu(x @ w1) * (x @ w3)) @ w2

def moe(h, w_router, router_bias, w_e1, w_e3, w_e2, w_s1, w_s3, w_s2):
    T = h.shape[0]
    dt = h.dtype
    scores = jax.nn.sigmoid(h.astype(jnp.float32) @ w_router.astype(jnp.float32))
    choice = scores + router_bias.astype(jnp.float32)
    grp = choice.reshape(T, N_GROUPS, N_EXPERTS // N_GROUPS)
    grp_score = jnp.sum(lax.top_k(grp, 2)[0], axis=-1)
    _, top_g = lax.top_k(grp_score, TOPK_GROUPS)
    gmask = jnp.sum(jax.nn.one_hot(top_g, N_GROUPS, dtype=jnp.float32), axis=1) > 0
    gmask = jnp.repeat(gmask, N_EXPERTS // N_GROUPS, axis=1)
    choice = jnp.where(gmask, choice, -jnp.inf)
    _, top_e = lax.top_k(choice, TOP_K)
    wts = jnp.take_along_axis(scores, top_e, axis=1)
    wts = wts / jnp.sum(wts, axis=-1, keepdims=True) * ROUTE_SCALE
    A = T * TOP_K
    e_flat = top_e.reshape(-1).astype(jnp.int32)
    tok_flat = jnp.repeat(jnp.arange(T, dtype=jnp.int32), TOP_K)
    w_flat = wts.reshape(-1)
    order = jnp.argsort(e_flat)
    e_s, tok_s, w_s = e_flat[order], tok_flat[order], w_flat[order]
    counts = jnp.bincount(e_flat, length=N_EXPERTS)
    starts = jnp.cumsum(counts) - counts
    nblk_e = (counts + EXPERT_BLOCK - 1) // EXPERT_BLOCK
    blk_end = jnp.cumsum(nblk_e)
    pad_starts = (blk_end - nblk_e) * EXPERT_BLOCK
    pos = pad_starts[e_s] + (jnp.arange(A, dtype=jnp.int32) - starts[e_s])
    n_blocks = -(-A // EXPERT_BLOCK) + N_EXPERTS
    R = n_blocks * EXPERT_BLOCK
    row_tok = jnp.zeros((R,), jnp.int32).at[pos].set(tok_s)
    row_w = jnp.zeros((R,), jnp.float32).at[pos].set(w_s)
    blk_expert = jnp.minimum(jnp.searchsorted(blk_end, jnp.arange(n_blocks), side='right'), N_EXPERTS - 1)

    def expert_block(args):
        tok, w, e = args
        xb = h[tok]
        return swiglu(xb, w_e1[e].astype(dt), w_e3[e].astype(dt), w_e2[e].astype(dt)) * w[:, None].astype(dt)

    out = lax.map(expert_block, (row_tok.reshape(n_blocks, EXPERT_BLOCK), row_w.reshape(n_blocks, EXPERT_BLOCK), blk_expert))
    routed = jax.ops.segment_sum(out.reshape(R, -1), row_tok, num_segments=T)
    shared = swiglu(h, w_s1.astype(dt), w_s3.astype(dt), w_s2.astype(dt))
    return shared + routed

def setup_inputs(seed: int = 0) -> dict:
    key = jax.random.key(seed)
    ks = iter(jax.random.split(key, 48))
    f32 = jnp.float32
    nrm = lambda shape, scale: jax.random.normal(next(ks), shape, f32) * scale
    gain = lambda shape: 1.0 + nrm(shape, 0.02)
    L = DEPTH
    nb = D_INNER // QKV_BLOCK
    b_if = jnp.concatenate([nrm((L, N_HEADS), 0.1), 3.0 + 3.0 * jax.random.uniform(next(ks), (L, N_HEADS), f32)], axis=-1)
    return {
        'x_prompt': nrm((BATCH, SEQ, D_MODEL), 1.0),
        'x_sample': nrm((DEC_BATCH, DEC_SEQ, D_MODEL), 1.0),
        'state_conv': nrm((L, DEC_BATCH, CONV_K - 1, D_CONV), 0.5),
        'state_mconv': nrm((L, DEC_BATCH, MCONV_K - 1, D_INNER), 1.0),
        'state_C': nrm((L, DEC_BATCH, N_HEADS, HEAD_DIM, HEAD_DIM), 0.05),
        'state_n': nrm((L, DEC_BATCH, N_HEADS, HEAD_DIM), 0.1),
        'state_m': nrm((L, DEC_BATCH, N_HEADS), 1.0),
        'meta_tokens': nrm((N_META, D_MODEL), 1.0),
        'ln_in_g': gain((D_MODEL,)),
        'ln_in_b': nrm((D_MODEL,), 0.02),
        'w_in': nrm((L, D_MODEL, N_IN), D_MODEL ** -0.5),
        'conv_w': nrm((L, CONV_K, D_CONV), CONV_K ** -0.5),
        'conv_b': nrm((L, D_CONV), 0.02),
        'conv_ln_g': gain((L, D_CONV)),
        'conv_ln_b': nrm((L, D_CONV), 0.02),
        'w_conv_out': nrm((L, D_CONV, D_MODEL), BETA * D_CONV ** -0.5),
        'mconv_w': nrm((L, MCONV_K, D_INNER), MCONV_K ** -0.5),
        'mconv_b': nrm((L, D_INNER), 0.02),
        'w_q': nrm((L, nb, QKV_BLOCK, QKV_BLOCK), QKV_BLOCK ** -0.5),
        'w_k': nrm((L, nb, QKV_BLOCK, QKV_BLOCK), QKV_BLOCK ** -0.5),
        'w_v': nrm((L, nb, QKV_BLOCK, QKV_BLOCK), BETA * QKV_BLOCK ** -0.5),
        'w_if': nrm((L, 3 * D_INNER, 2 * N_HEADS), (3 * D_INNER) ** -0.5),
        'b_if': b_if,
        'mh_ln_g': gain((L, D_INNER)),
        'skip': gain((L, D_INNER)),
        'w_m_down': nrm((L, D_INNER, D_MODEL), BETA * D_INNER ** -0.5),
        'w_o': nrm((L, D_MODEL, D_MODEL), BETA * D_MODEL ** -0.5),
        'ln1_g': gain((L, D_MODEL)),
        'ln1_b': nrm((L, D_MODEL), 0.02),
        'ln2_g': gain((L, D_MODEL)),
        'ln2_b': nrm((L, D_MODEL), 0.02),
        'w_router': nrm((L, D_MODEL, N_EXPERTS), D_MODEL ** -0.5),
        'router_bias': nrm((L, N_EXPERTS), 0.01),
        'w_e1': nrm((L, N_EXPERTS, D_MODEL, D_EXPERT), D_MODEL ** -0.5),
        'w_e3': nrm((L, N_EXPERTS, D_MODEL, D_EXPERT), D_MODEL ** -0.5),
        'w_e2': nrm((L, N_EXPERTS, D_EXPERT, D_MODEL), BETA * D_EXPERT ** -0.5),
        'w_s1': nrm((L, D_MODEL, D_SHARED), D_MODEL ** -0.5),
        'w_s3': nrm((L, D_MODEL, D_SHARED), D_MODEL ** -0.5),
        'w_s2': nrm((L, D_SHARED, D_MODEL), BETA * D_SHARED ** -0.5),
    }

def reference(x_prompt, x_sample, state_conv, state_mconv, state_C, state_n, state_m,
              meta_tokens, ln_in_g, ln_in_b, w_in, conv_w, conv_b, conv_ln_g, conv_ln_b, w_conv_out,
              mconv_w, mconv_b, w_q, w_k, w_v, w_if, b_if, mh_ln_g, skip, w_m_down, w_o,
              ln1_g, ln1_b, ln2_g, ln2_b, w_router, router_bias, w_e1, w_e3, w_e2, w_s1, w_s3, w_s2):
    f32 = jnp.float32
    B = x_prompt.shape[0]
    DB = x_sample.shape[0]
    meta = jnp.broadcast_to(meta_tokens.astype(x_prompt.dtype)[None], (B, N_META, D_MODEL))
    hp = layer_norm(jnp.concatenate([meta, x_prompt], axis=1), ln_in_g, ln_in_b)
    hs = layer_norm(x_sample, ln_in_g, ln_in_b)
    Lp = hp.shape[1]
    Ls = hs.shape[1]
    zc = jnp.zeros((B, CONV_K - 1, D_CONV), hp.dtype)
    zmc = jnp.zeros((B, MCONV_K - 1, D_INNER), hp.dtype)
    zC = jnp.zeros((B, N_HEADS, HEAD_DIM, HEAD_DIM), f32)
    zn = jnp.zeros((B, N_HEADS, HEAD_DIM), f32)
    zm = jnp.zeros((B, N_HEADS), f32)
    conv_p, mconv_p, C_p, n_p, m_p = [], [], [], [], []
    conv_s, mconv_s, C_s, n_s, m_s = [], [], [], [], []
    for l in range(DEPTH):
        mw = (w_in[l], conv_w[l], conv_b[l], conv_ln_g[l], conv_ln_b[l], w_conv_out[l], mconv_w[l], mconv_b[l],
              w_q[l], w_k[l], w_v[l], w_if[l], b_if[l], mh_ln_g[l], skip[l], w_m_down[l], w_o[l])
        op, cb, mb, C1, n1, m1 = mix_sublayer(hp, zc, zmc, zC, zn, zm, N_META, CHUNK, *mw)
        conv_p.append(cb); mconv_p.append(mb); C_p.append(C1); n_p.append(n1); m_p.append(m1)
        os_, cb, mb, C1, n1, m1 = mix_sublayer(hs, state_conv[l], state_mconv[l], state_C[l], state_n[l], state_m[l], 0, Ls, *mw)
        conv_s.append(cb); mconv_s.append(mb); C_s.append(C1); n_s.append(n1); m_s.append(m1)
        hp = layer_norm(ALPHA * hp + op, ln1_g[l], ln1_b[l])
        hs = layer_norm(ALPHA * hs + os_, ln1_g[l], ln1_b[l])
        ew = (w_router[l], router_bias[l], w_e1[l], w_e3[l], w_e2[l], w_s1[l], w_s3[l], w_s2[l])
        fp = moe(hp.reshape(B * Lp, D_MODEL), *ew).reshape(B, Lp, D_MODEL)
        fs = moe(hs.reshape(DB * Ls, D_MODEL), *ew).reshape(DB, Ls, D_MODEL)
        hp = layer_norm(ALPHA * hp + fp, ln2_g[l], ln2_b[l])
        hs = layer_norm(ALPHA * hs + fs, ln2_g[l], ln2_b[l])
    y_prompt = hp[:, N_META:]
    y_sample = hs
    return (y_prompt, y_sample,
            jnp.stack(conv_p), jnp.stack(mconv_p), jnp.stack(C_p), jnp.stack(n_p), jnp.stack(m_p),
            jnp.stack(conv_s), jnp.stack(mconv_s), jnp.stack(C_s), jnp.stack(n_s), jnp.stack(m_s))


_drawn_inputs = setup_inputs


def setup_inputs(seed=0):
    import zlib

    import numpy as np

    out = dict(_drawn_inputs(seed))
    spreads = {}
    factors = {'conv_ln_g': 9.007,
     'conv_ln_b': 7.967,
     'mh_ln_g': 8.914,
     'skip': 18.653,
     'ln2_g': 21.287,
     'ln2_b': 22.276}
    for name, (base, spread) in spreads.items():
        noise = np.random.default_rng([zlib.crc32(name.encode()), seed]).standard_normal(out[name].shape)
        drawn = base * np.exp(spread * noise) if base else spread * noise
        out[name] = __import__('jax').numpy.asarray(drawn.astype(out[name].dtype))
    for name, factor in factors.items():
        out[name] = (out[name] * factor).astype(out[name].dtype)
    return out
```

```python
from contextlib import ExitStack

import concourse.bass as bass
from concourse import mybir

F32 = mybir.dt.float32
I32 = mybir.dt.int32
ALU = mybir.AluOpType
ACT = mybir.ActivationFunctionType
AX = mybir.AxisListType

P = 128
D = 1024
SEQ, N_META = 256, 16
NSEQ, LSEQ = 8, 8
NS = NSEQ * LSEQ
NPR = N_META + SEQ
T = NS + NPR
TT = 112
NT = T // TT
KD = D // P
DI = 2 * D
KI = DI // P
NH, HD = 4, 512
HT = HD // P
CK, MK = 31, 4
NE, FE = 64, 256
NG, GE = 8, 8
ROUTE_SCALE = 2.5
ALPHA = 2.0 ** 0.25
EPS = 1e-5
NEG = -1.0e30
SCALE = HD ** -0.5
GLU_A, GLU_B, XM, OG, GA, GB = 0, D, 2 * D, 2 * D + DI, 2 * D + 2 * DI, 3 * D + 2 * DI
RING = 6
CR = 3


class Signal:

    def __init__(self, sem):
        self.sem, self.n = sem, 0

    def inc(self, ins, by=1):
        ins.then_inc(self.sem, by)
        self.n += by
        return self.n


def step(eng, sig, ins):
    eng.wait_ge(sig.sem, sig.inc(ins))


def mixer_groups():
    g = [("rows1", "v"), ("rows2", "v")]
    g += [(("hist", c), "a") for c in range(4)] + [("mhist", "a"), ("n0", "v")]
    g += [(("hT", i, c), "a" if c else "v") for i in range(NT) for c in range(2)]
    for c in range(2):
        g += [(("glu_b", 4 * c + j), "a") for j in range(4)] + [(("glu_a", 4 * c + j), "v") for j in range(4)]
    g += [(("xm", c), "a") for c in range(KI)]
    g += [(("ga", c), "a") for c in range(KD)]
    g += [(("us", c), "a") for c in range(2)] + [(("up", c), "a") for c in range(2)]
    g += [(("xs", c), "a") for c in range(4)] + [(("xp", c), "a") for c in range(4)]
    g += [("mean", "v"), ("var", "v")]
    g += [(("ya", c), "v") for c in range(KD)]
    g += [("gates", "v"), ("send", "v"), ("cols", "v")]
    for h in range(NH):
        g += [(("bc", h), "v")]
        g += [(("q", h, c), "a") for c in range(HT)] + [(("k", h, c), "a") for c in range(HT)]
        g += [(("kt", h, i), "a") for i in range(NT)] + [(("vt", h, i), "v") for i in range(NT)]
        g += [(("s", h, i), "v") for i in range(NT)]
        g += [(("num", h, i), "v") for i in range(1, NT)]
        g += [(("n1", h), "v")]
        g += [(("og", h, c), "a") for c in range(HT)]
        for s in range(NSEQ):
            g += [(("upd", h, s, c), "v") for c in range(HT)]
        g += [(("cp", h, c), "a") for c in range(HT)]
        g += [(("hh", h, i), "a") for i in range(NT)]
    g += [(("gb", c), "a") for c in range(KD)]
    g += [(("yb", c), "v") for c in range(KD)]
    g += [(("op", c, i), "v") for c in range(2) for i in range(NT)]
    return g


def weight_chunks():
    w = []
    for c in range(2):
        w += [("in", GLU_B + 512 * c, ("glu_b", 4 * c + 3)), ("in", GLU_A + 512 * c, ("glu_a", 4 * c + 3))]
    w += [("in", XM + 512 * c, ("xm", 4 * c + 3)) for c in range(4)]
    w += [("in", GA + 512 * c, ("ga", 4 * c + 3)) for c in range(2)]
    w += [("conv_out", 512 * c, ("ya", 4 * c + 3)) for c in range(2)]
    w += [("in", OG + 512 * h, ("og", h, HT - 1)) for h in range(NH)]
    w += [("in", GB + 512 * c, ("gb", 4 * c + 3)) for c in range(2)]
    w += [("down", 256 * c, ("yb", 2 * c + 1)) for c in range(4)]
    w += [("o", 512 * c, ("op", c, NT - 1)) for c in range(2)]
    return w


class Memory:

    def __init__(self, nc):
        self.nc, self.top, self.end = nc, (nc.sbuf_base + 63) // 64 * 64, {}

    def __call__(self, name, shape, at=None):
        n = 4
        for s in shape[1:]:
            n *= s
        n = (n + 31) // 32 * 32
        if at is None:
            at, self.top = self.top, self.top + n
        assert at + n <= self.nc.sbuf_usable_end, (name, at + n, self.nc.sbuf_usable_end)
        self.end[name] = at + n
        return self.nc.alloc_sbuf_tensor_at(name, shape, F32, offset=at)


def build(nc, I, O):
    ctx = ExitStack()
    with ctx:
        sb = Memory(nc)
        h = sb("h", [TT, NT, D])
        hT = sb("hT", [P, KD, T])
        ident = sb("ident", [P, P])
        ones = sb("ones", [P, P])
        shared = sb.top
        bank = [ctx.enter_context(nc.psum_tensor(f"bank{i}", [P, 512], F32)) for i in range(8)]
        lnstat = sb("lnstat", [TT, NT, 16])
        with ExitStack() as part:
            mixer(nc, ctx, part, sb, bank, I, O, h, hT, ident, ones, lnstat)
        sb.top = shared
        lnstat2 = sb("lnstat2", [TT, NT, 16])
        with ExitStack() as part:
            moe(nc, ctx, part, sb, bank, I, O, h, hT, ident, lnstat2)


def inverse_root(dve, nc, chain, y, x, t):
    v = nc.vector
    step(dve, chain, v.tensor_scalar(x, x, EPS, None, ALU.add))
    step(dve, chain, v.tensor_scalar(t.bitcast(I32), x.bitcast(I32), 1, None, ALU.logical_shift_right))
    step(dve, chain, v.tensor_scalar(y.bitcast(I32), t.bitcast(I32), -1.0, float(0x5F3759DF), ALU.mult, ALU.add))
    for _ in range(3):
        step(dve, chain, v.tensor_tensor(t, y, y, ALU.mult))
        step(dve, chain, v.scalar_tensor_tensor(out=t, in0=t, scalar=-0.5, in1=x, op0=ALU.mult, op1=ALU.mult))
        step(dve, chain, v.scalar_tensor_tensor(out=y, in0=t, scalar=1.5, in1=y, op0=ALU.add, op1=ALU.mult))


def layer_norm_rows(dve, nc, chain, stat, x, gain, bias):
    for c in range(2):
        step(dve, chain, nc.vector.bn_stats(stat[:, 6 * c:6 * c + 6], x[:, 512 * c:512 * c + 512]))
    step(dve, chain, nc.vector.bn_aggr(stat[:, 12:14], stat[:, 0:12].rearrange("p (c s) -> p c s", s=6)))
    inverse_root(dve, nc, chain, stat[:, 14:15], stat[:, 13:14], stat[:, 15:16])
    step(dve, chain, nc.vector.tensor_scalar(x, x, stat[:, 12:13], stat[:, 14:15], ALU.subtract, ALU.mult))
    if gain is not None:
        step(dve, chain, nc.vector.tensor_tensor(x, x, gain, ALU.mult))
        step(dve, chain, nc.vector.tensor_tensor(x, x, bias, ALU.add))


def mixer(nc, ctx, part, sb, bank, I, O, h, hT, ident, ones, lnstat):
    def sem(name):
        return ctx.enter_context(nc.semaphore(name))

    end = sb.end
    bmask = sb("bmask", [P, 32])
    negmask = sb("negmask", [TT, NT, T])
    sel = sb("sel", [NH, NH, P])
    seqmask = sb("seqmask", [NS, NSEQ])
    segmul = sb("segmul", [NH, T])
    segadd = sb("segadd", [NH, T])
    cc = sb("cc", [P, KD, 34])
    mc = sb("mc", [P, KI, 7])
    wqkv = sb("wqkv", [P, 3, KI, 4])
    n0T = sb("n0T", [P, HT, NSEQ * NH])
    n0rows = sb("n0rows", [NSEQ * NH, HD])
    m0row = sb("m0row", [NH, NSEQ])
    bif = sb("bif", [36, 1])
    acol = sb("acol", [TT, NT, 68])
    wend = sb("wend", [TT, NT, NH, 9])
    send9 = sb("send9", [9, NH])
    nmrow = sb("nmrow", [NH, T])
    srow = sb("srow", [NH, NS])
    sbq = sb("sbq", [P, NS])
    rden = sb("rden", [TT, 4])
    yaT = sb("yaT", [P, KD, T])
    cm = sb("cm", [P, KI, T])
    xm = sb("xm", [P, KI, T])
    wring = sb("wring", [P, 2, 4096])
    z = sb.top
    lng = sb("lng", [TT, D], at=end["sbq"] + 64)
    lnb = sb("lnb", [TT, D], at=end["lng"])
    u = sb("u", [P, KD, T], at=z)
    hist = sb("hist", [P, KD, NSEQ * (CK - 1)], at=end["u"])
    mhist = sb("mhist", [P, KI, NSEQ * (MK - 1)], at=end["hist"])
    ca = sb("ca", [P, KD, T], at=end["mhist"])
    sq = sb("sq", [P, KD, T], at=end["ca"])
    sg = sb("sg", [P, 4, T], at=end["sq"])
    wifx = sb("wifx", [P, 3, KI, 32], at=end["sg"])
    mif = sb("mif", [P, 2, KI, 36], at=end["wifx"])
    mtmp = sb("mtmp", [P, 2, KI, 8], at=end["mif"])
    us_o = sb("us_o", [NS, D], at=end["sg"])
    up_o = sb("up_o", [CK - 1, D], at=end["mtmp"])
    rows1 = sb("rows1", [34, D], at=end["mhist"])
    histr = sb("histr", [4 * (CK - 1), 2, D], at=end["rows1"])
    rows2 = sb("rows2", [7, DI], at=end["mtmp"])
    mhistr = sb("mhistr", [NSEQ * (MK - 1), DI], at=end["histr"])
    xs_o = sb("xs_o", [NS, DI], at=end["up_o"])
    xp_o = sb("xp_o", [MK - 1, DI], at=end["xs_o"])
    ptmp = sb("ptmp", [P, KI, NS], at=end["xp_o"])
    gr = sb("gr", [NH, 8, T], at=z)
    st = sb("st", [68, T], at=end["gr"])
    se9 = sb("se9", [NH, 9], at=end["st"])
    cring = sb("cring", [P, CR, HT, HD], at=z)
    qT = sb("qT", [P, HT, T], at=end["cring"])
    kT = sb("kT", [P, HT, T], at=end["qT"])
    gb = sb("gb", [P, KD, T], at=end["cring"])
    ktok = sb("ktok", [TT, NT, HD], at=end["kT"])
    vtok = sb("vtok", [TT, NT, HD], at=end["ktok"])
    pt = sb("pt", [TT, NT, T], at=end["vtok"])
    qm = sb("qm", [P, HT, NSEQ, NS], at=end["pt"])
    qs = sb("qs", [P, HT, NS], at=end["qm"])
    qn = sb("qn", [P, HT, NS], at=end["qs"])
    kwm = sb("kwm", [NS, 2, HD], at=end["qn"])
    hh = sb("hh", [TT, NT, HD], at=end["kwm"])
    wbd = sb("wbd", [P, 3, HT, P], at=end["kwm"])
    n0x = sb("n0x", [9, HD], at=end["hh"])
    n1o = sb("n1o", [9, HD], at=end["n0x"])
    ln1g = sb("ln1g", [TT, D], at=z)
    ln1b = sb("ln1b", [TT, D], at=end["ln1g"])
    ybt = sb("ybt", [P, T], at=end["ln1b"])

    groups = mixer_groups()
    place = {name: n for n, (name, _) in enumerate(groups)}
    assert len(place) == len(groups)
    reader = [r for _, r in groups]
    count = [reader[:n + 1].count(reader[n]) for n in range(len(groups))]
    full = sem("full")
    took = {"a": sem("act_took"), "v": sem("dve_took")}

    def moved(eng, name):
        n = place[name]
        eng.wait_ge(took[reader[n]], count[n])

    def computed(eng, name):
        eng.wait_ge(full, place[name] + 1)

    chunks = weight_chunks()
    wloaded = [sem("wloaded0"), sem("wloaded1")]
    names = ("x0", "x1", "x2", "lnp", "rows1", "rows2", "histr", "mhistr", "n0rows", "wqkv", "wifx", "small", "ln1")
    ld = {n: sem("ld_" + n) for n in names}
    consts = sem("consts")
    N_CONST = 6
    zeroed = sem("zeroed")
    normed = sem("normed")
    mixed_gates = sem("mixed_gates")
    conv_v, conv_p = sem("conv_v"), sem("conv_p")
    centered, conv_normed, conv_act = sem("centered"), sem("conv_normed"), sem("conv_act")
    mconv_v, mconv_p, cm_act = sem("mconv_v"), sem("mconv_p"), sem("cm_act")
    abs_f, soft_f, exp_in, exp_out, se9_set = (sem(n) for n in ("abs_f", "soft_f", "exp_in", "exp_out", "se9_set"))
    wends = sem("wends")
    wbd_ready, arg_ready, decay_ready, pt_ready, qm_ready = (
        sem(n) for n in ("wbd_ready", "arg_ready", "decay_ready", "pt_ready", "qm_ready"))
    den_full, num0_full, den_read, num0_read = (sem(n) for n in ("den_full", "num0_full", "den_read", "num0_read"))
    kwm_ready, kend_ready, hh_ready, hb_ready = (sem(n) for n in ("kwm_ready", "kend_ready", "hh_ready", "hb_ready"))
    c_loaded = [sem(f"c_loaded{i}") for i in range(CR)]
    c_stored = [sem(f"c_stored{i}") for i in range(CR)]
    c_new = sem("c_new")
    n0_loaded, n1_stored = sem("n0_loaded"), sem("n1_stored")
    gb_done, merged, embedded = sem("gb_done"), sem("merged"), sem("embedded")
    stored, kept = sem("stored"), sem("kept")
    m_ready = sem("m_ready")
    block = part.enter_context(nc.Block())

    @block.sync
    def _(sp):
        def chunk(n):
            kind, c, _ = chunks[n]
            if n >= 2:
                computed(sp, chunks[n - 2][2])
            dst = wring[:, n % 2, :]
            if kind == "down":
                src = I["w_m_down"][0, :, c:c + 256].rearrange("(k p) n -> p k n", p=P)
                dst = dst.rearrange("p (k n) -> p k n", k=KI)
            else:
                w = {"in": I["w_in"], "conv_out": I["w_conv_out"], "o": I["w_o"]}[kind]
                src = w[0, :, c:c + 512].rearrange("(k p) n -> p k n", p=P)
                dst = dst.rearrange("p (k n) -> p k n", k=KD)
            sp.dma_start(dst, src).then_inc(wloaded[n % 2], 16)

        xp = I["x_prompt"][0]
        sp.dma_start(h[0:64, 0, :], I["x_sample"].rearrange("b l d -> (b l) d")).then_inc(ld["x0"], 16)
        sp.dma_start(h[64:80, 0, :], I["meta_tokens"]).then_inc(ld["x0"], 16)
        sp.dma_start(h[80:112, 0, :], xp[0:32]).then_inc(ld["x0"], 16)
        sp.dma_start(lng[:, :], I["ln_in_g"].rearrange("(a n) -> a n", a=1).to_broadcast([TT, D])).then_inc(ld["lnp"], 16)
        sp.dma_start(lnb[:, :], I["ln_in_b"].rearrange("(a n) -> a n", a=1).to_broadcast([TT, D])).then_inc(ld["lnp"], 16)
        sp.dma_start(h[:, 1, :], xp[32:144]).then_inc(ld["x1"], 16)
        sp.dma_start(h[:, 2, :], xp[144:256]).then_inc(ld["x2"], 16)
        chunk(0)
        chunk(1)
        sp.dma_start(rows1[0:31, :], I["conv_w"][0]).then_inc(ld["rows1"], 16)
        for r, n in enumerate(("conv_b", "conv_ln_g", "conv_ln_b")):
            sp.dma_start(rows1[31 + r:32 + r, :], I[n]).then_inc(ld["rows1"], 16)
        sp.dma_start(rows2[0:4, :], I["mconv_w"][0]).then_inc(ld["rows2"], 16)
        for r, n in enumerate(("mconv_b", "skip", "mh_ln_g")):
            sp.dma_start(rows2[4 + r:5 + r, :], I[n]).then_inc(ld["rows2"], 16)
        sp.dma_start(histr[:, :, :], I["state_conv"][0].rearrange("(a b) r d -> (b r) a d", a=2)).then_inc(ld["histr"], 16)
        sp.dma_start(mhistr[:, :], I["state_mconv"][0].rearrange("b r d -> (b r) d")).then_inc(ld["mhistr"], 16)
        sp.dma_start(n0rows[:, :], I["state_n"][0].rearrange("b h d -> (b h) d")).then_inc(ld["n0rows"], 16)
        for m, n in enumerate(("w_q", "w_k", "w_v")):
            sp.dma_start(wqkv[:, m, :, :], I[n][0].rearrange("(t b) i o -> (b i) t o", b=32)).then_inc(ld["wqkv"], 16)
            src = I["w_if"][0, m * DI:(m + 1) * DI, :].rearrange("(t b o) j -> b t (o j)", b=32, o=4)
            for i in range(4):
                sp.dma_start(wifx[i:P:4, m, :, :], src).then_inc(ld["wifx"], 16)
        sp.dma_start(bif[0:4, :], I["b_if"][0:1, 0:4].rearrange("a b -> b a")).then_inc(ld["small"], 16)
        sp.dma_start(bif[32:36, :], I["b_if"][0:1, 4:8].rearrange("a b -> b a")).then_inc(ld["small"], 16)
        sp.dma_start(m0row[:, :], I["state_m"][0].rearrange("b h -> h b"),
                     allow_slow_non_contiguous=True).then_inc(ld["small"], 16)
        sp.dma_start(O["conv_s"][0, :, 0:CK - 1 - LSEQ, :], I["state_conv"][0, :, LSEQ:, :]).then_inc(kept, 16)
        for n in range(2, 14):
            chunk(n)
        for hd in range(NH):
            if hd == 0:
                sp.wait_ge(zeroed, 2)
                computed(sp, ("ya", KD - 1))
            else:
                sp.wait_ge(n1_stored, 16 * (2 * hd))
            sp.dma_start(n0x[0:8, :], I["state_n"][0, :, hd, :]).then_inc(n0_loaded, 16)
            for s in range(NSEQ):
                e = hd * 9 + s
                if e >= CR:
                    sp.wait_ge(c_stored[e % CR], 16 * (e // CR))
                sp.dma_start(cring[:, e % CR, :, :], I["state_C"][0, s, hd].rearrange("(k p) e -> p k e", p=P)
                             ).then_inc(c_loaded[e % CR], 16)
            chunk(14 + hd)
        for n in range(18, len(chunks)):
            chunk(n)
        for i in range(CR):
            sp.wait_ge(c_stored[i], 16 * (NH * 9 // CR))
        sp.dma_start(ln1g[:, :], I["ln1_g"].to_broadcast([TT, D])).then_inc(ld["ln1"], 16)
        sp.dma_start(ln1b[:, :], I["ln1_b"].to_broadcast([TT, D])).then_inc(ld["ln1"], 16)
        sp.wait_ge(kept, 16)

    @block.gpsimd
    def _(pool):
        chain = Signal(sem("pool_chain"))
        g = nc.gpsimd

        def go(ins):
            step(pool, chain, ins)

        go(g.memset(ident[:], 0.0))
        g.affine_select(out=ident[:, :], in_=ident[:, :], compare_op=ALU.not_equal, fill=1.0, base=0,
                        pattern=[[-1, P]], channel_multiplier=1).then_inc(consts, 1)
        g.memset(ones[:], 1.0).then_inc(consts, 1)
        g.memset(mif[:], 0.0).then_inc(zeroed, 1)
        go(g.memset(bmask[:], 1.0))
        go(g.affine_select(out=bmask[:, :], in_=bmask[:, :], compare_op=ALU.is_ge, fill=0.0, base=0,
                           pattern=[[-4, 32]], channel_multiplier=1))
        g.affine_select(out=bmask[:, :], in_=bmask[:, :], compare_op=ALU.is_ge, fill=0.0, base=3,
                        pattern=[[4, 32]], channel_multiplier=-1).then_inc(consts, 1)
        go(g.memset(seqmask[:], 1.0))
        go(g.affine_select(out=seqmask[:, :], in_=seqmask[:, :], compare_op=ALU.is_ge, fill=0.0, base=0,
                           pattern=[[-LSEQ, NSEQ]], channel_multiplier=1))
        go(g.affine_select(out=seqmask[:, :], in_=seqmask[:, :], compare_op=ALU.is_ge, fill=0.0, base=LSEQ - 1,
                           pattern=[[LSEQ, NSEQ]], channel_multiplier=-1))
        go(g.memset(sel[:], 0.0))
        g.affine_select(out=sel[:, :, :], in_=sel[:, :, :], compare_op=ALU.not_equal, fill=1.0, base=0,
                        pattern=[[-1, NH], [0, P]], channel_multiplier=1).then_inc(consts, 1)
        go(g.memset(negmask[:], 0.0))
        for i in range(NT):
            go(g.affine_select(out=negmask[:, i, :], in_=negmask[:, i, :], compare_op=ALU.is_ge, fill=NEG,
                               base=-TT * i, pattern=[[1, T]], channel_multiplier=-1))
        v = negmask[:, 0, 0:NS].rearrange("p (q j) -> p q j", j=LSEQ)
        go(g.affine_select(out=v, in_=v, compare_op=ALU.is_ge, fill=NEG, base=0,
                           pattern=[[-LSEQ, NSEQ], [0, LSEQ]], channel_multiplier=1))
        g.affine_select(out=negmask[:, 0, NS:T], in_=negmask[:, 0, NS:T], compare_op=ALU.is_ge, fill=NEG,
                        base=-NS, pattern=[[0, NPR]], channel_multiplier=1).then_inc(consts, 1)
        go(g.memset(segmul[:], 1.0))
        go(g.memset(segadd[:], 0.0))
        go(g.memset(segmul[:, 0:NS].rearrange("p (q j) -> p q j", j=LSEQ)[:, :, 0:1], 0.0))
        go(g.memset(segmul[:, NS:NS + 1], 0.0))
        go(g.memset(segadd[:, 0:NS].rearrange("p (q j) -> p q j", j=LSEQ)[:, :, 0:1], NEG))
        g.memset(segadd[:, NS:NS + 1], NEG).then_inc(consts, 1)

        moved(pool, ("hist", 3))
        moved(pool, ("glu_a", KD - 1))
        moved(pool, ("hT", 2, 1))
        def sample_conv(x, past, out, taps, k, nc_, bias):
            xv = x[:, :, 0:NS].rearrange("p c (q j) -> p c q j", j=LSEQ)
            ov = out[:, :, 0:NS].rearrange("p c (q j) -> p c q j", j=LSEQ)
            pv = past[:, :, :].rearrange("p c (q r) -> p c q r", r=k - 1)
            tv = ptmp[:, 0:nc_, :].rearrange("p c (q j) -> p c q j", j=LSEQ)

            def weight(r, j):
                return taps[:, :, r:r + 1].rearrange("p c (a b) -> p c a b", a=1).to_broadcast([P, nc_, NSEQ, j])

            go(g.tensor_tensor(ov, xv, weight(k - 1, LSEQ), ALU.mult))
            if bias is not None:
                go(g.tensor_tensor(ov, ov, weight(bias, LSEQ), ALU.add))
            for d in range(1, k):
                j = min(d, LSEQ)
                parts = [(0, j, pv[:, :, :, k - 1 - d:k - 1 - d + j])]
                if j < LSEQ:
                    parts.append((j, LSEQ - j, xv[:, :, :, 0:LSEQ - j]))
                for t0, n, src in parts:
                    go(g.tensor_tensor(tv[:, :, :, t0:t0 + n], src, weight(k - 1 - d, n), ALU.mult))
                go(g.tensor_tensor(ov, ov, tv, ALU.add))

        sample_conv(u, hist, ca, cc, CK, KD, 31)
        g.memset(srow[:], 0.0).then_inc(conv_p, 1)
        moved(pool, "mhist")
        moved(pool, ("xm", KI - 1))
        sample_conv(xm, mhist, cm, mc, MK, KI, None)
        g.memset(sbq[:], 0.0).then_inc(mconv_p, 1)

        moved(pool, ("xp", 3))
        n_st = 0
        for s in range(NSEQ):
            pool.dma_start(O["conv_s"][0, s, CK - 1 - LSEQ:, :], us_o[LSEQ * s:LSEQ * s + LSEQ, :]).then_inc(stored, 16)
            pool.dma_start(O["mconv_s"][0, s], xs_o[LSEQ * s + LSEQ - 3:LSEQ * s + LSEQ, :]).then_inc(stored, 16)
            n_st += 32
        pool.dma_start(O["conv_p"][0, 0], up_o[:, :]).then_inc(stored, 16)
        pool.dma_start(O["mconv_p"][0, 0], xp_o[:, :]).then_inc(stored, 16)
        n_st += 32
        pool.wait_ge(m_ready, 1)
        pool.dma_start(O["m_s"][0].rearrange("b h -> h b"),
                       gr[:, 6, 0:NS].rearrange("p (q j) -> p q j", j=LSEQ)[:, :, LSEQ - 1:LSEQ].rearrange("p q a -> p (q a)"),
                       allow_slow_non_contiguous=True).then_inc(stored, 16)
        pool.dma_start(O["m_p"].rearrange("a b h -> h (a b)"), gr[:, 6, T - 1:T]).then_inc(stored, 16)
        n_st += 32
        pool.wait_ge(stored, n_st)
        pool.wait_ge(wends, 1)
        go(g.memset(n0x[:], 0.0))
        g.memset(qm[:], 0.0).then_inc(zeroed, 1)
        for hd in range(NH):
            moved(pool, ("n1", hd))
            pool.dma_start(O["n_s"][0, :, hd, :], n1o[0:8, :]).then_inc(n1_stored, 16)
            pool.dma_start(O["n_p"][0, :, hd, :], n1o[8:9, :]).then_inc(n1_stored, 16)
            for s in range(NSEQ + 1):
                e = hd * 9 + s
                if s < NSEQ:
                    moved(pool, ("upd", hd, s, HT - 1))
                    dst = O["C_s"][0, s, hd]
                else:
                    moved(pool, ("cp", hd, HT - 1))
                    dst = O["C_p"][0, 0, hd]
                pool.dma_start(dst.rearrange("(k p) e -> p k e", p=P), cring[:, e % CR, :, :]).then_inc(c_stored[e % CR], 16)
        pool.wait_ge(n1_stored, 32 * NH)
        for i in range(CR):
            pool.wait_ge(c_stored[i], 16 * (NH * 9 // CR))

    @block.tensor
    def _(pe):
        state = [0, 0]
        mm, tr = nc.tensor.matmul, nc.tensor.transpose

        def opened(name):
            n = state[0]
            state[0] += 1
            assert place[name] == n, name
            if n >= RING:
                pe.wait_ge(took[reader[n - RING]], count[n - RING])
            return bank[n % RING]

        def chunk(kind, c):
            n = state[1]
            state[1] += 1
            assert chunks[n][:2] == (kind, c)
            pe.wait_ge(wloaded[n % 2], 16 * (n // 2 + 1))
            w = wring[:, n % 2, :]
            return w.rearrange("p (k n) -> p k n", k=KI if kind == "down" else KD)

        def project(w, j, b, src=hT, k=KD):
            for kk in range(k):
                last = mm(b[:, 0:T], w[:, kk, P * j:P * j + P], src[:, kk, :], start=(kk == 0), stop=(kk == k - 1))
            last.then_inc(full, 1)
            return last

        def turns(name, pieces):
            b = opened(name)
            for src, kk, m, col in pieces:
                last = tr(b[0:m, col:col + kk], src, ident[0:kk, 0:kk])
            last.then_inc(full, 1)

        pe.wait_ge(consts, 1)
        pe.wait_ge(ld["rows1"], 64)
        turns("rows1", [(rows1[:, P * c:P * c + P], 34, P, 34 * c) for c in range(KD)])
        pe.wait_ge(ld["rows2"], 64)
        turns("rows2", [(rows2[:, P * c:P * c + P], 7, P, 7 * c) for c in range(KI)])
        pe.wait_ge(ld["histr"], 16)
        for c in range(4):
            turns(("hist", c), [(histr[:, c // 2, P * (4 * (c % 2) + j):P * (4 * (c % 2) + j) + P], 120, P, 120 * j)
                                for j in range(4)])
        pe.wait_ge(ld["mhistr"], 16)
        turns("mhist", [(mhistr[:, P * c:P * c + P], 24, P, 24 * c) for c in range(KI)])
        pe.wait_ge(ld["n0rows"], 16)
        turns("n0", [(n0rows[:, P * c:P * c + P], 32, P, 32 * c) for c in range(HT)])
        for i in range(NT):
            pe.wait_ge(normed, i + 1)
            for c in range(2):
                turns(("hT", i, c), [(h[:, i, P * (4 * c + j):P * (4 * c + j) + P], TT, P, TT * j) for j in range(4)])
        moved(pe, ("hT", 2, 0))
        moved(pe, ("hT", 2, 1))
        for c in range(2):
            for nm, col in (("glu_b", GLU_B), ("glu_a", GLU_A)):
                w = chunk("in", col + 512 * c)
                for j in range(4):
                    project(w, j, opened((nm, 4 * c + j)))
        for c in range(4):
            w = chunk("in", XM + 512 * c)
            for j in range(4):
                project(w, j, opened(("xm", 4 * c + j)))
        for c in range(2):
            w = chunk("in", GA + 512 * c)
            for j in range(4):
                project(w, j, opened(("ga", 4 * c + j)))
        moved(pe, ("glu_a", KD - 1))
        for c in range(2):
            turns(("us", c), [(u[:, 4 * c + j, 0:NS], P, NS, P * j) for j in range(4)])
        for c in range(2):
            turns(("up", c), [(u[:, 4 * c + j, T - CK + 1:T], P, CK - 1, P * j) for j in range(4)])
        moved(pe, ("xm", KI - 1))
        for c in range(4):
            turns(("xs", c), [(xm[:, 4 * c + j, 0:NS], P, NS, P * j) for j in range(4)])
        for c in range(4):
            turns(("xp", c), [(xm[:, 4 * c + j, T - MK + 1:T], P, MK - 1, P * j) for j in range(4)])
        pe.wait_ge(conv_v, 1)
        pe.wait_ge(conv_p, 1)
        for name, src, sig in (("mean", ca, None), ("var", sq, centered)):
            b = opened(name)
            if sig is not None:
                pe.wait_ge(sig, 1)
            for k in range(KD):
                last = mm(b[:, 0:T], ones[:, :], src[:, k, :], start=(k == 0), stop=(k == KD - 1))
            last.then_inc(full, 1)
        pe.wait_ge(conv_act, KD)
        for c in range(2):
            w = chunk("conv_out", 512 * c)
            for j in range(4):
                project(w, j, opened(("ya", 4 * c + j)), src=ca)
        pe.wait_ge(mixed_gates, 1)
        pe.wait_ge(cm_act, KI)
        b = opened("gates")
        for k in range(2 * KI):
            last = mm(b[0:36, 0:T], mif[:, k // KI, k % KI, :], (cm, xm)[k // KI][:, k % KI, :],
                      start=(k == 0), stop=(k == 2 * KI - 1))
        last.then_inc(full, 1)
        pe.wait_ge(se9_set, 1)
        turns("send", [(se9[:, :], NH, 9, 0)])
        pe.wait_ge(exp_out, 3)
        turns("cols", [(st[:, TT * i:TT * i + TT], 68, TT, 68 * i) for i in range(NT)])

        for hd in range(NH):
            b = opened(("bc", hd))
            mm(b[:, 0:T], sel[:, hd, :], nmrow[:, :], start=True, stop=True)
            mm(b[:, T:T + NS], sel[:, hd, :], srow[:, :], start=True, stop=True).then_inc(full, 1)
            pe.wait_ge(wbd_ready, hd + 1)
            for m, nm in enumerate("qk"):
                for c in range(HT):
                    b = opened((nm, hd, c))
                    mm(b[:, 0:T], wbd[:, m, c, :], cm[:, HT * hd + c, :], start=True, stop=True).then_inc(full, 1)
            for m, nm, src in ((1, "kt", cm), (2, "vt", xm)):
                for i in range(NT):
                    b = opened((nm, hd, i))
                    for c in range(HT):
                        last = mm(b[0:TT, P * c:P * c + P], src[:, HT * hd + c, TT * i:TT * i + TT], wbd[:, m, c, :],
                                  start=True, stop=True)
                    last.then_inc(full, 1)
            moved(pe, ("k", hd, HT - 1))
            for i in range(NT):
                b = opened(("s", hd, i))
                for k in range(HT):
                    last = mm(b[0:TT, 0:T], kT[:, k, TT * i:TT * i + TT], qT[:, k, :], start=(k == 0), stop=(k == HT - 1))
                last.then_inc(full, 1)
            moved(pe, ("s", hd, NT - 1))
            pe.wait_ge(qm_ready, hd + 1)
            if hd:
                pe.wait_ge(den_read, hd)
                pe.wait_ge(num0_read, hd)
            for i in range(NT):
                for s in range(i + 1):
                    last = mm(bank[6][0:TT, i:i + 1], pt[:, s, TT * i:TT * i + TT], ones[0:TT, 0:1], start=(s == 0),
                              stop=(s == i))
                if i == 0:
                    for k in range(HT):
                        last = mm(bank[6][0:NS, 0:1], qn[:, k, :], ones[:, 0:1], start=False, stop=(k == HT - 1),
                                  skip_group_check=True)
            last.then_inc(den_full, 1)
            moved(pe, ("vt", hd, NT - 1))
            for i in range(1, NT):
                b = opened(("num", hd, i))
                for s in range(i + 1):
                    last = mm(b[0:TT, :], pt[:, s, TT * i:TT * i + TT], vtok[:, s, :], start=(s == 0), stop=(s == i))
                last.then_inc(full, 1)
            mm(bank[7][0:TT, :], pt[:, 0, 0:TT], vtok[:, 0, :], start=True, stop=True)
            moved(pe, ("kt", hd, NT - 1))
            b = opened(("n1", hd))
            for i in range(NT):
                last = mm(b[0:9, :], wend[:, i, hd, :], ktok[:, i, :], start=(i == 0), stop=(i == NT - 1))
            last.then_inc(full, 1)
            w = chunk("in", OG + 512 * hd)
            for j in range(4):
                project(w, j, opened(("og", hd, j)))
            for s in range(NSEQ):
                e = hd * 9 + s
                c0 = cring[:, e % CR, :, :]
                loads = sum(1 for x in range(e + 1) if x % CR == e % CR and x % 9 < 8)
                pe.wait_ge(c_loaded[e % CR], 16 * loads)
                for k in range(HT):
                    last = mm(bank[7][0:NS, :], qm[:, k, s, :], c0[:, k, :], start=False,
                              stop=(s == NSEQ - 1 and k == HT - 1), skip_group_check=True)
                if s == NSEQ - 1:
                    last.then_inc(num0_full, 1)
                pe.wait_ge(kwm_ready, NSEQ * hd + s + 1)
                for c in range(HT):
                    b = opened(("upd", hd, s, c))
                    mm(b[:, :], kwm[:, s % 2, P * c:P * c + P], vtok[0:NS, 0, :], start=True, stop=True).then_inc(full, 1)
            pe.wait_ge(kend_ready, hd + 1)
            for c in range(HT):
                b = opened(("cp", hd, c))
                for i in range(NT):
                    last = mm(b[:, :], ktok[:, i, P * c:P * c + P], vtok[:, i, :], start=(i == 0), stop=(i == NT - 1))
                last.then_inc(full, 1)
            for i in range(NT):
                pe.wait_ge(hh_ready, NT * hd + (i + 1 if i else NT))
                turns(("hh", hd, i), [(hh[:, i, P * j:P * j + P], TT, P, TT * j) for j in range(4)])
        for c in range(2):
            w = chunk("in", GB + 512 * c)
            for j in range(4):
                project(w, j, opened(("gb", 4 * c + j)))
        pe.wait_ge(hb_ready, NH)
        for c in range(4):
            w = chunk("down", 256 * c)
            for j in range(2):
                project(w, j, opened(("yb", 2 * c + j)), src=cm, k=KI)
        moved(pe, ("yb", KD - 1))
        pe.wait_ge(merged, KD)
        for c in range(2):
            w = chunk("o", 512 * c)
            for i in range(NT):
                b = opened(("op", c, i))
                for k in range(KD):
                    last = mm(b[0:TT, :], yaT[:, k, TT * i:TT * i + TT], w[:, k, :], start=(k == 0), stop=(k == KD - 1))
                last.then_inc(full, 1)
        assert state[0] == len(groups) and state[1] == len(chunks)

    @block.scalar
    def _(act):
        a = nc.scalar
        chain = Signal(sem("act_chain"))
        tk = Signal(took["a"])

        def take(name):
            n = place[name]
            assert reader[n] == "a" and tk.n == count[n] - 1, name
            act.wait_ge(full, n + 1)
            return bank[n % RING]

        for c in range(4):
            b = take(("hist", c))
            tk.inc(a.copy(hist[:, 4 * (c % 2):4 * (c % 2) + 4, 120 * (c // 2):120 * (c // 2) + 120],
                          b[:, 0:480].rearrange("p (c r) -> p c r", c=4)))
        b = take("mhist")
        tk.inc(a.copy(mhist[:, :, :], b[:, 0:384].rearrange("p (c r) -> p c r", c=KI)))
        for i in range(NT):
            b = take(("hT", i, 1))
            tk.inc(a.copy(hT[:, 4:8, TT * i:TT * i + TT], b[:, 0:448].rearrange("p (c r) -> p c r", c=4)))
        for c in range(KD):
            b = take(("glu_b", c))
            if c >= 4:
                moved(act, ("glu_a", c - 4))
            tk.inc(a.activation(sg[:, c % 4, :], b[:, 0:T], ACT.Sigmoid))
        for c in range(KI):
            b = take(("xm", c))
            tk.inc(a.copy(xm[:, c, :], b[:, 0:T]))
        for c in range(KD):
            b = take(("ga", c))
            tk.inc(a.activation(yaT[:, c, :], b[:, 0:T], ACT.Sigmoid))
        for nm, n, rows, dst in (("us", 2, NS, us_o), ("up", 2, CK - 1, up_o), ("xs", 4, NS, xs_o), ("xp", 4, MK - 1, xp_o)):
            for c in range(n):
                b = take((nm, c))
                tk.inc(a.copy(dst[0:rows, 512 * c:512 * c + 512], b[0:rows, :]))
        act.wait_ge(conv_normed, 1)
        for c in range(KD):
            a.activation(ca[:, c, :], ca[:, c, :], ACT.Silu, bias=cc[:, c, 33:34], scale=cc[:, c, 32:33]).then_inc(conv_act, 1)
        act.wait_ge(mconv_v, 1)
        act.wait_ge(mconv_p, 1)
        for c in range(KI):
            a.activation(cm[:, c, :], cm[:, c, :], ACT.Silu, bias=mc[:, c, 4:5]).then_inc(cm_act, 1)
        act.wait_ge(abs_f, 1)
        step(act, chain, a.activation(gr[:, 3, :], gr[:, 2, :], ACT.Exp, scale=-1.0))
        a.activation(gr[:, 3, :], gr[:, 3, :], ACT.Ln, bias=1.0).then_inc(soft_f, 1)
        act.wait_ge(exp_in, 1)
        a.activation(st[32:36, :], gr[:, 6, :], ACT.Exp, scale=-1.0).then_inc(exp_out, 1)
        a.activation(st[64:68, :], gr[:, 7, :], ACT.Exp).then_inc(exp_out, 1)
        a.activation(srow[:, :], gr[:, 0, 0:NS], ACT.Exp).then_inc(exp_out, 1)
        kw = Signal(kwm_ready)
        for hd in range(NH):
            if hd:
                act.wait_ge(hb_ready, hd)
            else:
                moved(act, "cols")
                act.wait_ge(wends, 1)
                act.wait_ge(stored, 16 * 20)
            for nm, dst in (("q", qT), ("k", kT)):
                for c in range(HT):
                    b = take((nm, hd, c))
                    tk.inc(a.copy(dst[:, c, :], b[:, 0:T]))
            for i in range(NT):
                b = take(("kt", hd, i))
                tk.inc(a.copy(ktok[:, i, :], b[0:TT, :]))
            for i in range(NT):
                act.wait_ge(arg_ready, NT * hd + i + 1)
                a.activation(pt[:, i, :], pt[:, i, :], ACT.Exp, bias=acol[:, i, hd:hd + 1]).then_inc(decay_ready, 1)
            for c in range(HT):
                b = take(("og", hd, c))
                tk.inc(a.activation(kT[:, c, :], b[:, 0:T], ACT.Sigmoid))
            for s in range(NSEQ):
                if s >= 2 or hd:
                    ps, ph = (s - 2, hd) if s >= 2 else (s + NSEQ - 2, hd - 1)
                    computed(act, ("upd", ph, ps, HT - 1))
                if s == 0:
                    moved(act, ("kt", hd, NT - 1))
                kw.inc(a.mul(kwm[:, s % 2, :], ktok[0:NS, 0, :], wend[0:NS, 0, hd, s:s + 1]))
            act.wait_ge(kw.sem, kw.n)
            for i in range(NT):
                step(act, chain, a.mul(ktok[:, i, :], ktok[:, i, :], wend[:, i, hd, 8:9]))
            a.sign(rden[0:1, 3:4], rden[0:1, 3:4]).then_inc(kend_ready, 1)
            e = hd * 9 + NSEQ
            if e >= CR:
                act.wait_ge(c_stored[e % CR], 16 * (e // CR))
            for c in range(HT):
                b = take(("cp", hd, c))
                tk.inc(a.copy(cring[:, e % CR, c, :], b[:, :]))
            act.wait_ge(qm_ready, hd + 1)
            for i in range(NT):
                b = take(("hh", hd, i))
                for j in range(HT):
                    ins = a.mul(qT[:, j, TT * i:TT * i + TT], b[:, TT * j:TT * j + TT], mc[:, HT * hd + j, 6:7])
                    (tk if j == HT - 1 else chain).inc(ins)
        act.wait_ge(hb_ready, NH)
        for c in range(KD):
            b = take(("gb", c))
            tk.inc(a.activation(gb[:, c, :], b[:, 0:T], ACT.Sigmoid))

    @block.vector
    def _(dve):
        v = nc.vector
        chain = Signal(sem("dve_chain"))
        tk = Signal(took["v"])

        def go(ins):
            step(dve, chain, ins)

        def take(name):
            n = place[name]
            assert reader[n] == "v" and tk.n == count[n] - 1, name
            dve.wait_ge(full, n + 1)
            return bank[n % RING]

        b = take("rows1")
        tk.inc(v.tensor_copy(cc[:, :, :], b[:, 0:272].rearrange("p (c r) -> p c r", c=KD)))
        b = take("rows2")
        tk.inc(v.tensor_copy(mc[:, :, :], b[:, 0:112].rearrange("p (c r) -> p c r", c=KI)))
        dve.wait_ge(ld["x0"], 48)
        dve.wait_ge(ld["lnp"], 32)
        nsig = Signal(normed)

        def norm_rows(i, gain, bias, sig):
            x, s = h[:, i, :], lnstat[:, i, :]
            layer_norm_rows(dve, nc, chain, s, x, None, None)
            go(v.tensor_tensor(x, x, gain, ALU.mult))
            sig.inc(v.tensor_tensor(x, x, bias, ALU.add))

        norm_rows(0, lng[:, :], lnb[:, :], nsig)
        b = take("n0")
        tk.inc(v.tensor_copy(n0T[:, :, :], b[:, 0:128].rearrange("p (c r) -> p c r", c=HT)))
        for i in range(NT):
            if i < NT - 1:
                dve.wait_ge(ld[f"x{i + 1}"], 16)
                norm_rows(i + 1, lng[:, :], lnb[:, :], nsig)
            b = take(("hT", i, 0))
            tk.inc(v.tensor_copy(hT[:, 0:4, TT * i:TT * i + TT], b[:, 0:448].rearrange("p (c r) -> p c r", c=4)))
        dve.wait_ge(ld["wqkv"], 48)
        dve.wait_ge(ld["wifx"], 16 * 12)
        dve.wait_ge(zeroed, 1)
        for m in range(3):
            for o in range(4):
                dst = mtmp[:, 0 if (o == 0 and m != 1) else 1, :, :]
                go(v.tensor_tensor(dst, wifx[:, m, :, 8 * o:8 * o + 8],
                                   wqkv[:, m, :, o:o + 1].to_broadcast([P, KI, 8]), ALU.mult))
                if o or m == 1:
                    go(v.tensor_tensor(mtmp[:, 0, :, :], mtmp[:, 0, :, :], mtmp[:, 1, :, :], ALU.add))
            if m:
                for j in range(2):
                    go(v.tensor_copy(mif[:, m - 1, :, 32 * j:32 * j + 4], mtmp[:, 0, :, 4 * j:4 * j + 4]))
        v.memset(lnstat[0:1, 0, 0:1], 0.0).then_inc(mixed_gates, 1)
        for c in range(KD):
            b = take(("glu_a", c))
            moved(dve, ("glu_b", c))
            tk.inc(v.tensor_tensor(u[:, c, :], b[:, 0:T], sg[:, c % 4, :], ALU.mult))
        moved(dve, ("hT", 2, 1))
        for c in range(KD):
            moved(dve, ("glu_a", c))
            chain.inc(v.tensor_scalar(ca[:, c, NS:T], u[:, c, NS:T], cc[:, c, CK - 1:CK], cc[:, c, 31:32], ALU.mult, ALU.add))
        for d in range(1, CK):
            for c in range(KD):
                dve.wait_ge(chain.sem, chain.n - KD + 1)
                chain.inc(v.scalar_tensor_tensor(out=ca[:, c, NS + d:T], in0=u[:, c, NS:T - d],
                                                 scalar=cc[:, c, CK - 1 - d:CK - d], in1=ca[:, c, NS + d:T],
                                                 op0=ALU.mult, op1=ALU.add))
        dve.wait_ge(chain.sem, chain.n)
        v.memset(lnstat[0:1, 0, 0:1], 0.0).then_inc(conv_v, 1)
        b = take("mean")
        step(dve, tk, v.tensor_scalar(sg[:, 0, :], b[:, 0:T], 1.0 / D, None, ALU.mult))
        go(v.tensor_tensor(ca[:, :, :], ca[:, :, :], sg[:, 0:1, :].to_broadcast([P, KD, T]), ALU.subtract))
        v.tensor_tensor(sq[:, :, :], ca[:, :, :], ca[:, :, :], ALU.mult).then_inc(centered, 1)
        moved(dve, ("xm", KI - 1))
        for d in range(MK):
            for c in range(KI):
                w = mc[:, c, MK - 1 - d:MK - d]
                if d == 0:
                    chain.inc(v.tensor_scalar(cm[:, c, NS:T], xm[:, c, NS:T], w, None, ALU.mult))
                    continue
                dve.wait_ge(chain.sem, chain.n - KI + 1)
                chain.inc(v.scalar_tensor_tensor(out=cm[:, c, NS + d:T], in0=xm[:, c, NS:T - d], scalar=w,
                                                 in1=cm[:, c, NS + d:T], op0=ALU.mult, op1=ALU.add))
            if d == 0:
                b = take("var")
                step(dve, tk, v.tensor_scalar(sg[:, 0, :], b[:, 0:T], 1.0 / D, None, ALU.mult))
                inverse_root(dve, nc, chain, sg[:, 1, :], sg[:, 0, :], sg[:, 2, :])
                v.tensor_tensor(ca[:, :, :], ca[:, :, :], sg[:, 1:2, :].to_broadcast([P, KD, T]),
                                ALU.mult).then_inc(conv_normed, 1)
        dve.wait_ge(chain.sem, chain.n)
        v.memset(lnstat[0:1, 0, 0:1], 0.0).then_inc(mconv_v, 1)
        for c in range(KD):
            b = take(("ya", c))
            moved(dve, ("ga", c))
            tk.inc(v.tensor_tensor(yaT[:, c, :], b[:, 0:T], yaT[:, c, :], ALU.mult))
        dve.wait_ge(ld["small"], 48)
        dve.wait_ge(consts, N_CONST)
        computed(dve, "gates")
        b = take("gates")
        go(v.tensor_scalar(gr[:, 5, :], b[0:4, 0:T], bif[0:4, :], None, ALU.add))
        step(dve, tk, v.tensor_scalar(gr[:, 1, :], b[32:36, 0:T], bif[32:36, :], None, ALU.add))
        v.scalar_tensor_tensor(out=gr[:, 2, :], in0=gr[:, 1, :], scalar=-1.0, in1=gr[:, 1, :], op0=ALU.mult,
                               op1=ALU.max).then_inc(abs_f, 1)
        go(v.memset(st[:], 0.0))
        go(v.memset(se9[:], 0.0))
        go(v.tensor_scalar(gr[:, 1, :], gr[:, 1, :], 0.0, None, ALU.min))
        dve.wait_ge(soft_f, 1)
        go(v.tensor_tensor(gr[:, 1, :], gr[:, 1, :], gr[:, 3, :], ALU.subtract))
        go(v.tensor_tensor_scan(gr[:, 4, :], segmul[:, :], gr[:, 1, :], 0.0, ALU.mult, ALU.add))
        go(v.tensor_tensor(gr[:, 5, :], gr[:, 5, :], gr[:, 4, :], ALU.subtract))
        go(v.tensor_copy(st[0:4, :], gr[:, 5, :]))
        go(v.tensor_copy(gr[:, 7, :], gr[:, 5, :]))
        s7 = gr[:, 7, 0:NS].rearrange("p (q j) -> p q j", j=LSEQ)
        go(v.tensor_tensor(s7[:, :, 0:1], s7[:, :, 0:1], m0row[:, :].rearrange("p (q a) -> p q a", a=1), ALU.max))
        go(v.tensor_scalar(gr[:, 7, NS:NS + 1], gr[:, 7, NS:NS + 1], 0.0, None, ALU.max))
        go(v.tensor_tensor_scan(gr[:, 3, :], segadd[:, :], gr[:, 7, :], 0.0, ALU.add, ALU.max))
        go(v.tensor_scalar(nmrow[:, :], gr[:, 3, :], -1.0, None, ALU.mult))
        step(dve, Signal(m_ready), v.tensor_tensor(gr[:, 6, :], gr[:, 4, :], gr[:, 3, :], ALU.add))
        M = gr[:, 3, 0:NS].rearrange("p (q j) -> p q j", j=LSEQ)
        a5 = gr[:, 5, 0:NS].rearrange("p (q j) -> p q j", j=LSEQ)
        go(v.tensor_tensor(s7, a5, M[:, :, LSEQ - 1:LSEQ].to_broadcast([NH, NSEQ, LSEQ]), ALU.subtract))
        go(v.tensor_scalar(gr[:, 7, NS:T], gr[:, 5, NS:T], gr[:, 3, T - 1:T], None, ALU.subtract))
        v.tensor_tensor(gr[:, 0, 0:NS].rearrange("p (q j) -> p q j", j=LSEQ),
                        m0row[:, :].rearrange("p (q a) -> p q a", a=1).to_broadcast([NH, NSEQ, LSEQ]), M,
                        ALU.subtract).then_inc(exp_in, 1)
        dve.wait_ge(exp_out, 3)
        v.tensor_copy(se9[:, 0:8].rearrange("p (q a) -> p q a", a=1),
                      srow[:, :].rearrange("p (q j) -> p q j", j=LSEQ)[:, :, LSEQ - 1:LSEQ]).then_inc(se9_set, 1)
        b = take("send")
        step(dve, tk, v.tensor_copy(send9[:, :], b[0:9, 0:4]))
        b = take("cols")
        go(v.memset(wend[:], 0.0))
        step(dve, tk, v.tensor_copy(acol[:, :, :], b[0:TT, 0:NT * 68].rearrange("p (i r) -> p i r", i=NT)))
        go(v.tensor_scalar(acol[:, :, 64:68], acol[:, :, 64:68], SCALE, None, ALU.mult))
        for hd in range(NH):
            go(v.tensor_scalar(wend[0:NS, 0, hd, 0:8], seqmask[:, :], acol[0:NS, 0, 64 + hd:65 + hd], None, ALU.mult))
        go(v.tensor_copy(wend[NS:TT, 0, :, 8], acol[NS:TT, 0, 64:68]))
        go(v.tensor_copy(wend[:, 1, :, 8], acol[:, 1, 64:68]))
        v.tensor_copy(wend[:, 2, :, 8], acol[:, 2, 64:68]).then_inc(wends, 1)
        dve.wait_ge(wends, 1)
        dve.wait_ge(stored, 16 * 20)

        wb, ar, pr, qr, dr, nr, hr, hb = (Signal(s) for s in (wbd_ready, arg_ready, pt_ready, qm_ready, den_read,
                                                              num0_read, hh_ready, hb_ready))
        for hd in range(NH):
            if hd:
                computed(dve, ("hh", hd - 1, NT - 1))
            for m in range(3):
                for c in range(HT):
                    ins = v.tensor_tensor(
                        wbd[:, m, c, :].rearrange("p (b o) -> p b o", o=4),
                        wqkv[:, m, HT * hd + c:HT * hd + c + 1, :].to_broadcast([P, 32, 4]),
                        bmask[:, :].rearrange("p (b o) -> p b o", o=1).to_broadcast([P, 32, 4]), ALU.mult)
                    if m == 2 and c == HT - 1:
                        dve.wait_ge(chain.sem, chain.n)
                        wb.inc(ins)
                    else:
                        chain.inc(ins)
            b = take(("bc", hd))
            go(v.tensor_copy(sbq[:, :], b[:, T:T + NS]))
            for i in range(NT):
                ar.inc(v.tensor_tensor(pt[:, i, :], b[0:TT, 0:T], negmask[:, i, :], ALU.add))
            step(dve, tk, v.tensor_copy(rden[:, 3:4], b[0:TT, 0:1]))
            moved(dve, ("q", hd, HT - 1))
            dve.wait_ge(zeroed, 2)
            for k in range(HT):
                chain.inc(v.tensor_tensor(qs[:, k, :], qT[:, k, 0:NS], sbq[:, :], ALU.mult))
            dve.wait_ge(chain.sem, chain.n)
            for k in range(HT):
                q3 = qs[:, k, :].rearrange("p (q j) -> p q j", j=LSEQ)
                diag = bass.AP(qm[:, k, :, :].tensor, qm[:, k, :, :].offset, [list(x) for x in qm[:, k, :, :].ap][:1] + [[NS + LSEQ, NSEQ], [1, LSEQ]])
                chain.inc(v.tensor_copy(diag, q3))
                n3 = n0T[:, k, :].rearrange("p (q g) -> p q g", g=NH)[:, :, hd:hd + 1].to_broadcast([P, NSEQ, LSEQ])
                chain.inc(v.tensor_tensor(qn[:, k, :].rearrange("p (q j) -> p q j", j=LSEQ), q3, n3, ALU.mult))
            dve.wait_ge(chain.sem, chain.n)
            qr.inc(v.tensor_copy(rden[0:1, 3:4], rden[0:1, 3:4]))
            for i in range(NT):
                b = take(("vt", hd, i))
                tk.inc(v.tensor_copy(vtok[:, i, :], b[0:TT, :]))
            for i in range(NT):
                b = take(("s", hd, i))
                dve.wait_ge(decay_ready, NT * hd + i + 1)
                tk.inc(v.scalar_tensor_tensor(out=pt[:, i, :], in0=b[0:TT, 0:T], scalar=SCALE, in1=pt[:, i, :],
                                              op0=ALU.mult, op1=ALU.mult))
            dve.wait_ge(den_full, hd + 1)
            step(dve, dr, v.tensor_copy(rden[:, 0:NT], bank[6][0:TT, 0:NT]))
            go(v.scalar_tensor_tensor(out=rden[:, 0:NT], in0=rden[:, 0:NT], scalar=-1.0, in1=rden[:, 0:NT],
                                      op0=ALU.mult, op1=ALU.max))
            go(v.tensor_tensor(rden[:, 0:NT], rden[:, 0:NT], acol[:, :, 32 + hd], ALU.max))
            go(v.reciprocal(rden[:, 0:NT], rden[:, 0:NT]))

            def finish(i, b, read):
                x, s = hh[:, i, :], lnstat[:, i, :]
                step(dve, read, v.tensor_scalar(x, b[0:TT, :], rden[:, i:i + 1], None, ALU.mult))
                go(v.bn_stats(s[:, 0:6], x))
                go(v.bn_aggr(s[:, 12:14], s[:, 0:6]))
                inverse_root(dve, nc, chain, s[:, 14:15], s[:, 13:14], s[:, 15:16])
                hr.inc(v.tensor_scalar(x, x, s[:, 12:13], s[:, 14:15], ALU.subtract, ALU.mult))

            for i in range(1, NT):
                finish(i, take(("num", hd, i)), tk)
            b = take(("n1", hd))
            dve.wait_ge(n0_loaded, 16 * (hd + 1))
            if hd:
                dve.wait_ge(n1_stored, 32 * hd)
            tk.inc(v.scalar_tensor_tensor(out=n1o[:, :], in0=n0x[:, :], scalar=send9[:, hd:hd + 1], in1=b[0:9, :],
                                          op0=ALU.mult, op1=ALU.add))
            for s in range(NSEQ):
                e = hd * 9 + s
                for c in range(HT):
                    b = take(("upd", hd, s, c))
                    cv = cring[:, e % CR, c, :]
                    tk.inc(v.scalar_tensor_tensor(out=cv, in0=cv, scalar=sbq[:, LSEQ * s + LSEQ - 1:LSEQ * s + LSEQ],
                                                  in1=b[:, :], op0=ALU.mult, op1=ALU.add))
            dve.wait_ge(num0_full, hd + 1)
            finish(0, bank[7], nr)
            moved(dve, ("hh", hd, NT - 1))
            moved(dve, ("og", hd, HT - 1))
            for c in range(HT):
                x = cm[:, HT * hd + c, :]
                go(v.scalar_tensor_tensor(out=x, in0=x, scalar=mc[:, HT * hd + c, 5:6], in1=qT[:, c, :],
                                          op0=ALU.mult, op1=ALU.add))
                ins = v.tensor_tensor(x, x, kT[:, c, :], ALU.mult)
                if c == HT - 1:
                    dve.wait_ge(chain.sem, chain.n)
                    hb.inc(ins)
                else:
                    chain.inc(ins)
        mg = Signal(merged)
        for c in range(KD):
            b = take(("yb", c))
            moved(dve, ("gb", c))
            step(dve, tk, v.tensor_tensor(gb[:, c, :], b[:, 0:T], gb[:, c, :], ALU.mult))
            mg.inc(v.tensor_tensor(yaT[:, c, :], yaT[:, c, :], gb[:, c, :], ALU.add))
        for c in range(2):
            for i in range(NT):
                b = take(("op", c, i))
                x = h[:, i, 512 * c:512 * c + 512]
                tk.inc(v.scalar_tensor_tensor(out=x, in0=x, scalar=ALPHA, in1=b[0:TT, :], op0=ALU.mult, op1=ALU.add))
        dve.wait_ge(tk.sem, tk.n)
        dve.wait_ge(ld["ln1"], 32)
        es = Signal(embedded)
        for i in range(NT):
            norm_rows(i, ln1g[:, :], ln1b[:, :], es)
        assert tk.n == reader.count("v")


def moe(nc, ctx, part, sb, bank, I, O, h, hT, ident, lnstat):
    def sem(name):
        return ctx.enter_context(nc.semaphore(name))

    ws = [[sb(f"we1_{s}", [P, KD, FE]), sb(f"we3_{s}", [P, KD, FE]), sb(f"we2_{s}", [P, 2, D])] for s in range(2)]
    acc = sb("acc", [TT, NT, D])
    wr = sb("wr", [P, KD, NE])
    rbias = sb("rbias", [TT, NE])
    lg = sb("lg", [TT, D])
    lb = sb("lb", [TT, D])
    sc = sb("sc", [TT, NT, NE])
    ch = sb("ch", [TT, NT, NE])
    wt = sb("wt", [TT, NT, NE])
    t8 = sb("t8", [TT, NG, 8])
    gs = sb("gs", [TT, 4, 8])
    rs = sb("rs", [TT, 2])
    silu = sb("silu", [P, 2, T])
    act_ = sb("act_", [P, 2, T])

    loaded = [sem("exp_loaded0"), sem("exp_loaded1")]
    parm, turned, hT_set = sem("moe_parm"), sem("turned"), sem("hT_set")
    logits, scored, silued, gated, gu_full, out_full, out_took = (
        sem(n) for n in ("logits", "scored", "silued", "gated", "gu_full", "out_full", "out_took"))
    weights_set, normed2, y_stored, hT_a = sem("weights_set"), sem("normed2"), sem("y_stored"), sem("hT_a")
    block = part.enter_context(nc.Block())
    srcs = (I["w_e1"], I["w_e3"], I["w_e2"])
    shared = (I["w_s1"], I["w_s3"], I["w_s2"])

    def load(sp, s, srcs3):
        for j, src in enumerate(srcs3):
            sp.dma_start(ws[s][j][:, :, :], src.rearrange("(p k) n -> p k n", p=P)).then_inc(loaded[s], 16)

    @block.sync
    def _(sp):
        sp.dma_start(wr[:, :, :], I["w_router"][0].rearrange("(p k) n -> p k n", p=P)).then_inc(parm, 16)
        sp.dma_start(rbias[:, :], I["router_bias"].to_broadcast([TT, NE])).then_inc(parm, 16)
        sp.dma_start(lg[:, :], I["ln2_g"].to_broadcast([TT, D])).then_inc(parm, 16)
        sp.dma_start(lb[:, :], I["ln2_b"].to_broadcast([TT, D])).then_inc(parm, 16)
        load(sp, 0, [w[0] for w in shared])
        load(sp, 1, [w[0, 0] for w in srcs])
        with sp.Fori(1, NE - 1, 2) as e:
            for s in range(2):
                sp.wait_ge(out_full, (e + s) * 6)
                load(sp, s, [w[0, e + s] for w in srcs])
        sp.wait_ge(out_full, 6 * (NE - 1))
        load(sp, 0, [w[0, NE - 1] for w in srcs])

    @block.tensor
    def _(pe):
        mm = nc.tensor.matmul
        tn = Signal(turned)
        for i in range(NT):
            for c in range(2):
                n = 2 * i + c
                for j in range(4):
                    k = 4 * c + j
                    last = nc.tensor.transpose(bank[n][:, TT * j:TT * j + TT], h[:, i, k:D:KD], ident[0:TT, 0:TT])
                tn.inc(last)
        pe.wait_ge(hT_set, 3)
        pe.wait_ge(hT_a, 3)
        pe.wait_ge(parm, 64)
        for i in range(NT):
            for k in range(KD):
                last = mm(bank[6][0:TT, NE * i:NE * i + NE], hT[:, k, TT * i:TT * i + TT], wr[:, k, :],
                          start=(k == 0), stop=(k == KD - 1))
        last.then_inc(logits, 1)

        def passes(n, s, nl):
            w1, w3, w2 = ws[s]
            pe.wait_ge(loaded[s], nl)
            for j in range(2):
                for w, b in ((w1, bank[j]), (w3, bank[2 + j])):
                    for k in range(KD):
                        last = mm(b[:, 0:T], w[:, k, j:FE:2], hT[:, k, :], start=(k == 0), stop=(k == KD - 1))
                    last.then_inc(gu_full, 1)
            pe.wait_ge(gated, n * 2 + 2)
            for x in range(6):
                i, c = x // 2, x % 2
                t = n * 6 + x
                if not (isinstance(n, int) and n == 0 and x < 4):
                    pe.wait_ge(out_took, t - 3)
                for j in range(2):
                    last = mm(bank[4 + (x + 2 * s) % 4][0:TT, :], act_[:, j, TT * i:TT * i + TT],
                              w2[:, j, 512 * c:512 * c + 512], start=(j == 0), stop=(j == 1))
                last.then_inc(out_full, 1)

        pe.wait_ge(scored, 1)
        passes(0, 0, 48)
        with pe.Fori(0, (NE - 1) // 2) as r:
            for s in (1, 0):
                passes(r * 2 + (1 if s else 2), s, r * 48 + (48 if s else 96))
        passes(NE - 1, 1, 48 * (NE // 2))
        passes(NE, 0, 48 * (NE // 2 + 1))

    @block.scalar
    def _(act):
        a = nc.scalar
        for i in range(NT):
            act.wait_ge(turned, 2 * i + 2)
            a.copy(hT[:, 4:8, TT * i:TT * i + TT],
                   bank[2 * i + 1][:, 0:448].rearrange("p (c r) -> p c r", c=4)).then_inc(hT_a, 1)
        act.wait_ge(logits, 1)
        a.activation(sc[:, :, :], bank[6][0:TT, 0:NT * NE].rearrange("p (i e) -> p i e", i=NT),
                     ACT.Sigmoid).then_inc(scored, 1)

        def silus(n, s):
            for j in range(2):
                act.wait_ge(gu_full, n * 4 + 2 * j + 1)
                if not (isinstance(n, int) and n == 0):
                    act.wait_ge(gated, n * 2 + j - 1)
                a.activation(silu[:, j, :], bank[j][:, 0:T], ACT.Silu).then_inc(silued, 1)

        silus(0, 0)
        with act.Fori(0, (NE - 1) // 2) as r:
            for s in (1, 0):
                silus(r * 2 + (1 if s else 2), s)
        silus(NE - 1, 1)
        silus(NE, 0)
        for i in range(NT):
            act.wait_ge(normed2, i + 1)
            if i == 0:
                act.dma_start(O["y_sample"].rearrange("b l d -> (b l) d"), h[0:NS, 0, :]).then_inc(y_stored, 16)
                act.dma_start(O["y_prompt"][0, 0:32, :], h[80:112, 0, :]).then_inc(y_stored, 16)
            else:
                act.dma_start(O["y_prompt"][0, TT * i - 80:TT * i + 32, :], h[:, i, :]).then_inc(y_stored, 16)
        act.wait_ge(y_stored, 64)

    @block.vector
    def _(dve):
        v = nc.vector
        chain = Signal(sem("moe_chain"))

        def go(ins):
            step(dve, chain, ins)

        for i in range(NT):
            dve.wait_ge(turned, 2 * i + 1)
            v.tensor_copy(hT[:, 0:4, TT * i:TT * i + TT],
                          bank[2 * i][:, 0:448].rearrange("p (c r) -> p c r", c=4)).then_inc(hT_set, 1)
        dve.wait_ge(scored, 1)
        dve.wait_ge(parm, 64)
        for i in range(NT):
            s, c, w = sc[:, i, :], ch[:, i, :], wt[:, i, :]
            go(v.tensor_tensor(c, s, rbias[:, :], ALU.add))
            for g in range(NG):
                go(v.max(t8[:, g, :], c[:, GE * g:GE * g + GE]))
            go(v.tensor_tensor(gs[:, 0, :], t8[:, :, 0], t8[:, :, 1], ALU.add))
            go(v.max(gs[:, 1, :], gs[:, 0, :]))
            go(v.memset(gs[:, 1, 4:8], -NEG))
            go(v.match_replace(gs[:, 2, :], gs[:, 1, :], gs[:, 0, :], NEG))
            go(v.tensor_tensor(gs[:, 3, :], gs[:, 0, :], gs[:, 2, :], ALU.is_equal))
            go(v.tensor_scalar(gs[:, 3, :], gs[:, 3, :], NEG, None, ALU.mult))
            go(v.tensor_tensor(c.rearrange("p (g e) -> p g e", e=GE), c.rearrange("p (g e) -> p g e", e=GE),
                               gs[:, 3, :].rearrange("p (g a) -> p g a", a=1).to_broadcast([TT, NG, GE]), ALU.add))
            go(v.max(t8[:, 0, :], c))
            go(v.match_replace(w, t8[:, 0, :], c, 2 * NEG))
            go(v.tensor_tensor(w, c, w, ALU.not_equal))
            go(v.tensor_tensor(w, w, s, ALU.mult))
            go(v.tensor_reduce(rs[:, 0:1], w, AX.X, ALU.add))
            go(v.reciprocal(rs[:, 1:2], rs[:, 0:1]))
            go(v.tensor_scalar(w, w, rs[:, 1:2], ROUTE_SCALE, ALU.mult, ALU.mult))

        def passes(n, s, col):
            for j in range(2):
                dve.wait_ge(silued, n * 2 + j + 1)
                dve.wait_ge(gu_full, n * 4 + 2 * j + 2)
                if not (isinstance(n, int) and n == 0):
                    dve.wait_ge(out_full, n * 6)
                v.tensor_tensor(act_[:, j, :], silu[:, j, :], bank[2 + j][:, 0:T], ALU.mult).then_inc(gated, 1)
            for x in range(6):
                i, c = x // 2, x % 2
                dve.wait_ge(out_full, n * 6 + x + 1)
                b = bank[4 + (x + 2 * s) % 4][0:TT, :]
                o = acc[:, i, 512 * c:512 * c + 512]
                if col is None:
                    v.tensor_copy(o, b).then_inc(out_took, 1)
                else:
                    dve.wait_ge(out_took, n * 6 + x - 5)
                    v.scalar_tensor_tensor(out=o, in0=b, scalar=wt[:, i, bass.ds(col, 1)], in1=o, op0=ALU.mult,
                                           op1=ALU.add).then_inc(out_took, 1)

        passes(0, 0, None)
        with dve.Fori(0, (NE - 1) // 2) as r:
            for s in (1, 0):
                passes(r * 2 + (1 if s else 2), s, r * 2 + (0 if s else 1))
        passes(NE - 1, 1, NE - 2)
        passes(NE, 0, NE - 1)
        dve.wait_ge(out_took, 6 * (NE + 1))
        ns = Signal(normed2)
        for i in range(NT):
            x = h[:, i, :]
            go(v.scalar_tensor_tensor(out=x, in0=x, scalar=ALPHA, in1=acc[:, i, :], op0=ALU.mult, op1=ALU.add))
            layer_norm_rows(dve, nc, chain, lnstat[:, i, :], x, None, None)
            go(v.tensor_tensor(x, x, lg[:, :], ALU.mult))
            ns.inc(v.tensor_tensor(x, x, lb[:, :], ALU.add))


_INS = ["x_prompt", "x_sample", "state_conv", "state_mconv", "state_C", "state_n", "state_m", "meta_tokens",
        "ln_in_g", "ln_in_b", "w_in", "conv_w", "conv_b", "conv_ln_g", "conv_ln_b", "w_conv_out", "mconv_w", "mconv_b",
        "w_q", "w_k", "w_v", "w_if", "b_if", "mh_ln_g", "skip", "w_m_down", "w_o", "ln1_g", "ln1_b", "ln2_g", "ln2_b",
        "w_router", "router_bias", "w_e1", "w_e3", "w_e2", "w_s1", "w_s3", "w_s2"]
_OUTS = {"y_prompt": (1, SEQ, D), "y_sample": (NSEQ, LSEQ, D), "conv_p": (1, 1, CK - 1, D),
         "mconv_p": (1, 1, MK - 1, DI), "C_p": (1, 1, NH, HD, HD), "n_p": (1, 1, NH, HD), "m_p": (1, 1, NH),
         "conv_s": (1, NSEQ, CK - 1, D), "mconv_s": (1, NSEQ, MK - 1, DI), "C_s": (1, NSEQ, NH, HD, HD),
         "n_s": (1, NSEQ, NH, HD), "m_s": (1, NSEQ, NH)}


def kernel(**inputs):
    import numpy as _np
    import concourse.bacc as _bacc
    from concourse import mybir as _mybir
    from concourse.bass_utils import run_bass_kernel_spmd as _run

    nc = _bacc.Bacc("TRN2", target_bir_lowering=False, num_devices=1)
    arrays, I, O = {}, {}, {}
    for name in _INS:
        a = _np.ascontiguousarray(inputs[name])
        arrays[f"in_{name}"] = a
        I[name] = nc.dram_tensor(f"in_{name}", a.shape, _mybir.dt.from_np(a.dtype), kind="ExternalInput").ap()
    for name, shape in _OUTS.items():
        O[name] = nc.dram_tensor(f"out_{name}", shape, _mybir.dt.float32, kind="ExternalOutput").ap()
    build(nc, I, O)
    r = _run(nc, [arrays], core_ids=[0])
    return tuple(r.results[0][f"out_{name}"] for name in _OUTS)
```

```python
from contextlib import ExitStack

import concourse.bass as bass
from concourse import mybir

F32 = mybir.dt.float32
I32 = mybir.dt.int32
BF16 = mybir.dt.bfloat16
ALU = mybir.AluOpType
ACT = mybir.ActivationFunctionType
AX = mybir.AxisListType

P = 128
D = 1024
SEQ, N_META = 256, 16
NSEQ, LSEQ = 8, 8
NS = NSEQ * LSEQ
NPR = N_META + SEQ
T = NS + NPR
TT = 112
NT = T // TT
KD = D // P
DI = 2 * D
KI = DI // P
NH, HD = 4, 512
HT = HD // P
CK, MK = 31, 4
NE, FE = 64, 256
NG, GE = 8, 8
TOP_K = 8
CAP = 64
MAXB = -(-T // CAP)
MAXO = T * TOP_K // (CAP + 1)
YROWS = (NE + MAXO + MAXB + 3) * CAP
NG_BUF = 8
ROUTE_SCALE = 2.5
ALPHA = 2.0 ** 0.25
EPS = 1e-5
NEG = -1.0e30
SCALE = HD ** -0.5
GLU_A, GLU_B, XM, OG, GA, GB = 0, D, 2 * D, 2 * D + DI, 2 * D + 2 * DI, 3 * D + 2 * DI
RING = 6
CR = 3


class Signal:

    def __init__(self, sem):
        self.sem, self.n = sem, 0

    def inc(self, ins, by=1):
        ins.then_inc(self.sem, by)
        self.n += by
        return self.n


def step(eng, sig, ins):
    eng.wait_ge(sig.sem, sig.inc(ins))


def mixer_groups():
    g = [("rows1", "v"), ("rows2", "v")]
    g += [(("hist", c), "a") for c in range(4)] + [("mhist", "a"), ("n0", "v")]
    g += [(("hT", i, c), "a" if c else "v") for i in range(NT) for c in range(2)]
    for c in range(2):
        g += [(("glu_b", 4 * c + j), "a") for j in range(4)] + [(("glu_a", 4 * c + j), "v") for j in range(4)]
    g += [(("xm", c), "a") for c in range(KI)]
    g += [(("ga", c), "a") for c in range(KD)]
    g += [(("us", c), "a") for c in range(2)] + [(("up", c), "a") for c in range(2)]
    g += [(("xs", c), "a") for c in range(4)] + [(("xp", c), "a") for c in range(4)]
    g += [("mean", "v"), ("var", "v")]
    g += [(("ya", c), "v") for c in range(KD)]
    g += [("gates", "v"), ("send", "v"), ("cols", "v")]
    for h in range(NH):
        g += [(("bc", h), "v")]
        g += [(("q", h, c), "a") for c in range(HT)] + [(("k", h, c), "a") for c in range(HT)]
        g += [(("kt", h, i), "a") for i in range(NT)] + [(("vt", h, i), "v") for i in range(NT)]
        g += [(("s", h, i), "v") for i in range(NT)]
        g += [(("num", h, i), "v") for i in range(1, NT)]
        g += [(("n1", h), "v")]
        g += [(("og", h, c), "a") for c in range(HT)]
        for s in range(NSEQ):
            g += [(("upd", h, s, c), "v") for c in range(HT)]
        g += [(("cp", h, c), "a") for c in range(HT)]
        g += [(("hh", h, i), "a") for i in range(NT)]
    g += [(("gb", c), "a") for c in range(KD)]
    g += [(("yb", c), "v") for c in range(KD)]
    g += [(("op", c, i), "v") for c in range(2) for i in range(NT)]
    return g


def weight_chunks():
    w = []
    for c in range(2):
        w += [("in", GLU_B + 512 * c, ("glu_b", 4 * c + 3)), ("in", GLU_A + 512 * c, ("glu_a", 4 * c + 3))]
    w += [("in", XM + 512 * c, ("xm", 4 * c + 3)) for c in range(4)]
    w += [("in", GA + 512 * c, ("ga", 4 * c + 3)) for c in range(2)]
    w += [("conv_out", 512 * c, ("ya", 4 * c + 3)) for c in range(2)]
    w += [("in", OG + 512 * h, ("og", h, HT - 1)) for h in range(NH)]
    w += [("in", GB + 512 * c, ("gb", 4 * c + 3)) for c in range(2)]
    w += [("down", 256 * c, ("yb", 2 * c + 1)) for c in range(4)]
    w += [("o", 512 * c, ("op", c, NT - 1)) for c in range(2)]
    return w


class Memory:

    def __init__(self, nc):
        self.nc, self.top, self.end = nc, (nc.sbuf_base + 63) // 64 * 64, {}

    def __call__(self, name, shape, at=None, dt=F32):
        n = 2 if dt == BF16 else 4
        for s in shape[1:]:
            n *= s
        n = (n + 31) // 32 * 32
        if at is None:
            at, self.top = self.top, self.top + n
        assert at + n <= self.nc.sbuf_usable_end, (name, at + n, self.nc.sbuf_usable_end)
        self.end[name] = at + n
        return self.nc.alloc_sbuf_tensor_at(name, shape, dt, offset=at)


def build(nc, I, O):
    ctx = ExitStack()
    with ctx:
        sb = Memory(nc)
        h = sb("h", [TT, NT, D])
        hT = sb("hT", [P, KD, T])
        ident = sb("ident", [P, P])
        ones = sb("ones", [P, P])
        shared = sb.top
        bank = [ctx.enter_context(nc.psum_tensor(f"bank{i}", [P, 512], F32)) for i in range(8)]
        lnstat = sb("lnstat", [TT, NT, 16])
        ybuf = nc.dram_tensor("expert_rows", (YROWS, D), F32, kind="Internal").ap()
        with ExitStack() as part:
            mixer(nc, ctx, part, sb, bank, I, O, ybuf, h, hT, ident, ones, lnstat)
        sb.top = shared
        lnstat2 = sb("lnstat2", [TT, NT, 16])
        with ExitStack() as part:
            moe(nc, ctx, part, sb, bank, I, O, ybuf, h, hT, ident, ones, lnstat2)


def inverse_root(dve, nc, chain, y, x, t):
    v = nc.vector
    step(dve, chain, v.tensor_scalar(x, x, EPS, None, ALU.add))
    step(dve, chain, v.tensor_scalar(t.bitcast(I32), x.bitcast(I32), 1, None, ALU.logical_shift_right))
    step(dve, chain, v.tensor_scalar(y.bitcast(I32), t.bitcast(I32), -1.0, float(0x5F3759DF), ALU.mult, ALU.add))
    for _ in range(3):
        step(dve, chain, v.tensor_tensor(t, y, y, ALU.mult))
        step(dve, chain, v.scalar_tensor_tensor(out=t, in0=t, scalar=-0.5, in1=x, op0=ALU.mult, op1=ALU.mult))
        step(dve, chain, v.scalar_tensor_tensor(out=y, in0=t, scalar=1.5, in1=y, op0=ALU.add, op1=ALU.mult))


def layer_norm_rows(dve, nc, chain, stat, x):
    for c in range(2):
        step(dve, chain, nc.vector.bn_stats(stat[:, 6 * c:6 * c + 6], x[:, 512 * c:512 * c + 512]))
    step(dve, chain, nc.vector.bn_aggr(stat[:, 12:14], stat[:, 0:12].rearrange("p (c s) -> p c s", s=6)))
    inverse_root(dve, nc, chain, stat[:, 14:15], stat[:, 13:14], stat[:, 15:16])
    step(dve, chain, nc.vector.tensor_scalar(x, x, stat[:, 12:13], stat[:, 14:15], ALU.subtract, ALU.mult))


def mixer(nc, ctx, part, sb, bank, I, O, ybuf, h, hT, ident, ones, lnstat):
    def sem(name):
        return ctx.enter_context(nc.semaphore(name))

    end = sb.end
    bmask = sb("bmask", [P, 32])
    negmask = sb("negmask", [TT, NT, T])
    sel = sb("sel", [NH, NH, P])
    seqmask = sb("seqmask", [NS, NSEQ])
    segmul = sb("segmul", [NH, T])
    segadd = sb("segadd", [NH, T])
    cc = sb("cc", [P, KD, 34])
    mc = sb("mc", [P, KI, 7])
    wqkv = sb("wqkv", [P, 3, KI, 4])
    n0T = sb("n0T", [P, HT, NSEQ * NH])
    n0rows = sb("n0rows", [NSEQ * NH, HD])
    m0row = sb("m0row", [NH, NSEQ])
    bif = sb("bif", [36, 1])
    acol = sb("acol", [TT, NT, 68])
    wend = sb("wend", [TT, NT, NH, 9])
    send9 = sb("send9", [9, NH])
    nmrow = sb("nmrow", [NH, T])
    srow = sb("srow", [NH, NS])
    sbq = sb("sbq", [P, NS])
    rden = sb("rden", [TT, 4])
    yaT = sb("yaT", [P, KD, T])
    cm = sb("cm", [P, KI, T])
    xm = sb("xm", [P, KI, T])
    wring = sb("wring", [P, 2, 4096])
    z = sb.top
    lng = sb("lng", [TT, D], at=end["sbq"] + 64)
    lnb = sb("lnb", [TT, D], at=end["lng"])
    u = sb("u", [P, KD, T], at=z)
    hist = sb("hist", [P, KD, NSEQ * (CK - 1)], at=end["u"])
    mhist = sb("mhist", [P, KI, NSEQ * (MK - 1)], at=end["hist"])
    ca = sb("ca", [P, KD, T], at=end["mhist"])
    sq = sb("sq", [P, KD, T], at=end["ca"])
    sg = sb("sg", [P, 4, T], at=end["sq"])
    wifx = sb("wifx", [P, 3, KI, 32], at=end["sg"])
    mif = sb("mif", [P, 2, KI, 36], at=end["wifx"])
    mtmp = sb("mtmp", [P, 2, KI, 8], at=end["mif"])
    us_o = sb("us_o", [NS, D], at=end["sg"])
    up_o = sb("up_o", [CK - 1, D], at=end["mtmp"])
    rows1 = sb("rows1", [34, D], at=end["mhist"])
    histr = sb("histr", [4 * (CK - 1), 2, D], at=end["rows1"])
    rows2 = sb("rows2", [7, DI], at=end["mtmp"])
    mhistr = sb("mhistr", [NSEQ * (MK - 1), DI], at=end["histr"])
    xs_o = sb("xs_o", [NS, DI], at=end["up_o"])
    xp_o = sb("xp_o", [MK - 1, DI], at=end["xs_o"])
    ptmp = sb("ptmp", [P, KI, NS], at=end["xp_o"])
    gr = sb("gr", [NH, 8, T], at=z)
    st = sb("st", [68, T], at=end["gr"])
    se9 = sb("se9", [NH, 9], at=end["st"])
    cring = sb("cring", [P, CR, HT, HD], at=z)
    qT = sb("qT", [P, HT, T], at=end["cring"])
    kT = sb("kT", [P, HT, T], at=end["qT"])
    gb = sb("gb", [P, KD, T], at=end["cring"])
    ktok = sb("ktok", [TT, NT, HD], at=end["kT"])
    vtok = sb("vtok", [TT, NT, HD], at=end["ktok"])
    pt = sb("pt", [TT, NT, T], at=end["vtok"])
    qm = sb("qm", [P, HT, NSEQ, NS], at=end["pt"])
    qs = sb("qs", [P, HT, NS], at=end["qm"])
    qn = sb("qn", [P, HT, NS], at=end["qs"])
    kwm = sb("kwm", [NS, 2, HD], at=end["qn"])
    hh = sb("hh", [TT, NT, HD], at=end["kwm"])
    wbd = sb("wbd", [P, 3, HT, P], at=end["kwm"])
    n0x = sb("n0x", [9, HD], at=end["hh"])
    n1o = sb("n1o", [9, HD], at=end["n0x"])
    ln1g = sb("ln1g", [TT, D], at=z)
    ln1b = sb("ln1b", [TT, D], at=end["ln1g"])
    ybt = sb("ybt", [P, T], at=end["ln1b"])

    groups = mixer_groups()
    place = {name: n for n, (name, _) in enumerate(groups)}
    assert len(place) == len(groups)
    reader = [r for _, r in groups]
    count = [reader[:n + 1].count(reader[n]) for n in range(len(groups))]
    full = sem("full")
    took = {"a": sem("act_took"), "v": sem("dve_took")}

    def moved(eng, name):
        n = place[name]
        eng.wait_ge(took[reader[n]], count[n])

    def computed(eng, name):
        eng.wait_ge(full, place[name] + 1)

    chunks = weight_chunks()
    wloaded = [sem("wloaded0"), sem("wloaded1")]
    names = ("x0", "x1", "x2", "lnp", "rows1", "rows2", "histr", "mhistr", "n0rows", "wqkv", "wifx", "small", "ln1")
    ld = {n: sem("ld_" + n) for n in names}
    consts = sem("consts")
    N_CONST = 6
    zeroed = sem("zeroed")
    normed = sem("normed")
    mixed_gates = sem("mixed_gates")
    conv_v, conv_p = sem("conv_v"), sem("conv_p")
    centered, conv_normed, conv_act = sem("centered"), sem("conv_normed"), sem("conv_act")
    mconv_v, mconv_p, cm_act = sem("mconv_v"), sem("mconv_p"), sem("cm_act")
    abs_f, soft_f, exp_in, exp_out, se9_set = (sem(n) for n in ("abs_f", "soft_f", "exp_in", "exp_out", "se9_set"))
    wends = sem("wends")
    wbd_ready, arg_ready, decay_ready, pt_ready, qm_ready = (
        sem(n) for n in ("wbd_ready", "arg_ready", "decay_ready", "pt_ready", "qm_ready"))
    den_full, num0_full, den_read, num0_read = (sem(n) for n in ("den_full", "num0_full", "den_read", "num0_read"))
    kwm_ready, kend_ready, hh_ready, hb_ready = (sem(n) for n in ("kwm_ready", "kend_ready", "hh_ready", "hb_ready"))
    c_loaded = [sem(f"c_loaded{i}") for i in range(CR)]
    c_stored = [sem(f"c_stored{i}") for i in range(CR)]
    c_new = sem("c_new")
    n0_loaded, n1_stored = sem("n0_loaded"), sem("n1_stored")
    gb_done, merged, embedded = sem("gb_done"), sem("merged"), sem("embedded")
    stored, kept, filled = sem("stored"), sem("kept"), sem("filled")
    m_ready = sem("m_ready")
    block = part.enter_context(nc.Block())

    @block.sync
    def _(sp):
        def chunk(n):
            kind, c, _ = chunks[n]
            if n >= 2:
                computed(sp, chunks[n - 2][2])
            dst = wring[:, n % 2, :]
            if kind == "down":
                src = I["w_m_down"][0, :, c:c + 256].rearrange("(k p) n -> p k n", p=P)
                dst = dst.rearrange("p (k n) -> p k n", k=KI)
            else:
                w = {"in": I["w_in"], "conv_out": I["w_conv_out"], "o": I["w_o"]}[kind]
                src = w[0, :, c:c + 512].rearrange("(k p) n -> p k n", p=P)
                dst = dst.rearrange("p (k n) -> p k n", k=KD)
            sp.dma_start(dst, src).then_inc(wloaded[n % 2], 16)

        xp = I["x_prompt"][0]
        sp.dma_start(h[0:64, 0, :], I["x_sample"].rearrange("b l d -> (b l) d")).then_inc(ld["x0"], 16)
        sp.dma_start(h[64:80, 0, :], I["meta_tokens"]).then_inc(ld["x0"], 16)
        sp.dma_start(h[80:112, 0, :], xp[0:32]).then_inc(ld["x0"], 16)
        sp.dma_start(lng[:, :], I["ln_in_g"].rearrange("(a n) -> a n", a=1).to_broadcast([TT, D])).then_inc(ld["lnp"], 16)
        sp.dma_start(lnb[:, :], I["ln_in_b"].rearrange("(a n) -> a n", a=1).to_broadcast([TT, D])).then_inc(ld["lnp"], 16)
        sp.dma_start(h[:, 1, :], xp[32:144]).then_inc(ld["x1"], 16)
        sp.dma_start(h[:, 2, :], xp[144:256]).then_inc(ld["x2"], 16)
        chunk(0)
        chunk(1)
        sp.dma_start(rows1[0:31, :], I["conv_w"][0]).then_inc(ld["rows1"], 16)
        for r, n in enumerate(("conv_b", "conv_ln_g", "conv_ln_b")):
            sp.dma_start(rows1[31 + r:32 + r, :], I[n]).then_inc(ld["rows1"], 16)
        sp.dma_start(rows2[0:4, :], I["mconv_w"][0]).then_inc(ld["rows2"], 16)
        for r, n in enumerate(("mconv_b", "skip", "mh_ln_g")):
            sp.dma_start(rows2[4 + r:5 + r, :], I[n]).then_inc(ld["rows2"], 16)
        sp.dma_start(histr[:, :, :], I["state_conv"][0].rearrange("(a b) r d -> (b r) a d", a=2)).then_inc(ld["histr"], 16)
        sp.dma_start(mhistr[:, :], I["state_mconv"][0].rearrange("b r d -> (b r) d")).then_inc(ld["mhistr"], 16)
        sp.dma_start(n0rows[:, :], I["state_n"][0].rearrange("b h d -> (b h) d")).then_inc(ld["n0rows"], 16)
        for m, n in enumerate(("w_q", "w_k", "w_v")):
            sp.dma_start(wqkv[:, m, :, :], I[n][0].rearrange("(t b) i o -> (b i) t o", b=32)).then_inc(ld["wqkv"], 16)
            src = I["w_if"][0, m * DI:(m + 1) * DI, :].rearrange("(t b o) j -> b t (o j)", b=32, o=4)
            for i in range(4):
                sp.dma_start(wifx[i:P:4, m, :, :], src).then_inc(ld["wifx"], 16)
        sp.dma_start(bif[0:4, :], I["b_if"][0:1, 0:4].rearrange("a b -> b a")).then_inc(ld["small"], 16)
        sp.dma_start(bif[32:36, :], I["b_if"][0:1, 4:8].rearrange("a b -> b a")).then_inc(ld["small"], 16)
        sp.dma_start(m0row[:, :], I["state_m"][0].rearrange("b h -> h b"),
                     allow_slow_non_contiguous=True).then_inc(ld["small"], 16)
        sp.dma_start(O["conv_s"][0, :, 0:CK - 1 - LSEQ, :], I["state_conv"][0, :, LSEQ:, :]).then_inc(kept, 16)
        for n in range(2, 14):
            chunk(n)
        for hd in range(NH):
            if hd == 0:
                sp.wait_ge(zeroed, 2)
                computed(sp, ("ya", KD - 1))
            else:
                sp.wait_ge(n1_stored, 16 * (2 * hd))
            sp.dma_start(n0x[0:8, :], I["state_n"][0, :, hd, :]).then_inc(n0_loaded, 16)
            for s in range(NSEQ):
                e = hd * 9 + s
                if e >= CR:
                    sp.wait_ge(c_stored[e % CR], 16 * (e // CR))
                sp.dma_start(cring[:, e % CR, :, :], I["state_C"][0, s, hd].rearrange("(k p) e -> p k e", p=P)
                             ).then_inc(c_loaded[e % CR], 16)
            chunk(14 + hd)
        for n in range(18, len(chunks)):
            chunk(n)
        for i in range(CR):
            sp.wait_ge(c_stored[i], 16 * (NH * 9 // CR))
        sp.dma_start(ln1g[:, :], I["ln1_g"].to_broadcast([TT, D])).then_inc(ld["ln1"], 16)
        sp.dma_start(ln1b[:, :], I["ln1_b"].to_broadcast([TT, D])).then_inc(ld["ln1"], 16)
        sp.wait_ge(kept, 16)

    @block.gpsimd
    def _(pool):
        chain = Signal(sem("pool_chain"))
        g = nc.gpsimd

        def go(ins):
            step(pool, chain, ins)

        go(g.memset(ident[:], 0.0))
        g.affine_select(out=ident[:, :], in_=ident[:, :], compare_op=ALU.not_equal, fill=1.0, base=0,
                        pattern=[[-1, P]], channel_multiplier=1).then_inc(consts, 1)
        g.memset(ones[:], 1.0).then_inc(consts, 1)
        g.memset(mif[:], 0.0).then_inc(zeroed, 1)
        go(g.memset(bmask[:], 1.0))
        go(g.affine_select(out=bmask[:, :], in_=bmask[:, :], compare_op=ALU.is_ge, fill=0.0, base=0,
                           pattern=[[-4, 32]], channel_multiplier=1))
        g.affine_select(out=bmask[:, :], in_=bmask[:, :], compare_op=ALU.is_ge, fill=0.0, base=3,
                        pattern=[[4, 32]], channel_multiplier=-1).then_inc(consts, 1)
        go(g.memset(seqmask[:], 1.0))
        go(g.affine_select(out=seqmask[:, :], in_=seqmask[:, :], compare_op=ALU.is_ge, fill=0.0, base=0,
                           pattern=[[-LSEQ, NSEQ]], channel_multiplier=1))
        go(g.affine_select(out=seqmask[:, :], in_=seqmask[:, :], compare_op=ALU.is_ge, fill=0.0, base=LSEQ - 1,
                           pattern=[[LSEQ, NSEQ]], channel_multiplier=-1))
        go(g.memset(sel[:], 0.0))
        g.affine_select(out=sel[:, :, :], in_=sel[:, :, :], compare_op=ALU.not_equal, fill=1.0, base=0,
                        pattern=[[-1, NH], [0, P]], channel_multiplier=1).then_inc(consts, 1)
        go(g.memset(negmask[:], 0.0))
        for i in range(NT):
            go(g.affine_select(out=negmask[:, i, :], in_=negmask[:, i, :], compare_op=ALU.is_ge, fill=NEG,
                               base=-TT * i, pattern=[[1, T]], channel_multiplier=-1))
        v = negmask[:, 0, 0:NS].rearrange("p (q j) -> p q j", j=LSEQ)
        go(g.affine_select(out=v, in_=v, compare_op=ALU.is_ge, fill=NEG, base=0,
                           pattern=[[-LSEQ, NSEQ], [0, LSEQ]], channel_multiplier=1))
        g.affine_select(out=negmask[:, 0, NS:T], in_=negmask[:, 0, NS:T], compare_op=ALU.is_ge, fill=NEG,
                        base=-NS, pattern=[[0, NPR]], channel_multiplier=1).then_inc(consts, 1)
        go(g.memset(segmul[:], 1.0))
        go(g.memset(segadd[:], 0.0))
        go(g.memset(segmul[:, 0:NS].rearrange("p (q j) -> p q j", j=LSEQ)[:, :, 0:1], 0.0))
        go(g.memset(segmul[:, NS:NS + 1], 0.0))
        go(g.memset(segadd[:, 0:NS].rearrange("p (q j) -> p q j", j=LSEQ)[:, :, 0:1], NEG))
        g.memset(segadd[:, NS:NS + 1], NEG).then_inc(consts, 1)

        moved(pool, ("hist", 3))
        moved(pool, ("glu_a", KD - 1))
        moved(pool, ("hT", 2, 1))
        def sample_conv(x, past, out, taps, k, nc_, bias):
            xv = x[:, :, 0:NS].rearrange("p c (q j) -> p c q j", j=LSEQ)
            ov = out[:, :, 0:NS].rearrange("p c (q j) -> p c q j", j=LSEQ)
            pv = past[:, :, :].rearrange("p c (q r) -> p c q r", r=k - 1)
            tv = ptmp[:, 0:nc_, :].rearrange("p c (q j) -> p c q j", j=LSEQ)

            def weight(r, j):
                return taps[:, :, r:r + 1].rearrange("p c (a b) -> p c a b", a=1).to_broadcast([P, nc_, NSEQ, j])

            go(g.tensor_tensor(ov, xv, weight(k - 1, LSEQ), ALU.mult))
            if bias is not None:
                go(g.tensor_tensor(ov, ov, weight(bias, LSEQ), ALU.add))
            for d in range(1, k):
                j = min(d, LSEQ)
                parts = [(0, j, pv[:, :, :, k - 1 - d:k - 1 - d + j])]
                if j < LSEQ:
                    parts.append((j, LSEQ - j, xv[:, :, :, 0:LSEQ - j]))
                for t0, n, src in parts:
                    go(g.tensor_tensor(tv[:, :, :, t0:t0 + n], src, weight(k - 1 - d, n), ALU.mult))
                go(g.tensor_tensor(ov, ov, tv, ALU.add))

        sample_conv(u, hist, ca, cc, CK, KD, 31)
        g.memset(srow[:], 0.0).then_inc(conv_p, 1)
        moved(pool, "mhist")
        moved(pool, ("xm", KI - 1))
        sample_conv(xm, mhist, cm, mc, MK, KI, None)
        g.memset(sbq[:], 0.0).then_inc(mconv_p, 1)

        moved(pool, ("xp", 3))
        n_st = 0
        for s in range(NSEQ):
            pool.dma_start(O["conv_s"][0, s, CK - 1 - LSEQ:, :], us_o[LSEQ * s:LSEQ * s + LSEQ, :]).then_inc(stored, 16)
            pool.dma_start(O["mconv_s"][0, s], xs_o[LSEQ * s + LSEQ - 3:LSEQ * s + LSEQ, :]).then_inc(stored, 16)
            n_st += 32
        pool.dma_start(O["conv_p"][0, 0], up_o[:, :]).then_inc(stored, 16)
        pool.dma_start(O["mconv_p"][0, 0], xp_o[:, :]).then_inc(stored, 16)
        n_st += 32
        pool.wait_ge(m_ready, 1)
        pool.dma_start(O["m_s"][0].rearrange("b h -> h b"),
                       gr[:, 6, 0:NS].rearrange("p (q j) -> p q j", j=LSEQ)[:, :, LSEQ - 1:LSEQ].rearrange("p q a -> p (q a)"),
                       allow_slow_non_contiguous=True).then_inc(stored, 16)
        pool.dma_start(O["m_p"].rearrange("a b h -> h (a b)"), gr[:, 6, T - 1:T]).then_inc(stored, 16)
        n_st += 32
        pool.wait_ge(stored, n_st)
        pool.wait_ge(wends, 1)
        go(g.memset(n0x[:], 0.0))
        g.memset(qm[:], 0.0).then_inc(zeroed, 1)
        for hd in range(NH):
            moved(pool, ("n1", hd))
            pool.dma_start(O["n_s"][0, :, hd, :], n1o[0:8, :]).then_inc(n1_stored, 16)
            pool.dma_start(O["n_p"][0, :, hd, :], n1o[8:9, :]).then_inc(n1_stored, 16)
            for s in range(NSEQ + 1):
                e = hd * 9 + s
                if s < NSEQ:
                    moved(pool, ("upd", hd, s, HT - 1))
                    dst = O["C_s"][0, s, hd]
                else:
                    moved(pool, ("cp", hd, HT - 1))
                    dst = O["C_p"][0, 0, hd]
                pool.dma_start(dst.rearrange("(k p) e -> p k e", p=P), cring[:, e % CR, :, :]).then_inc(c_stored[e % CR], 16)
        pool.wait_ge(n1_stored, 32 * NH)
        for i in range(CR):
            pool.wait_ge(c_stored[i], 16 * (NH * 9 // CR))

    @block.tensor
    def _(pe):
        state = [0, 0]
        mm, tr = nc.tensor.matmul, nc.tensor.transpose

        def opened(name):
            n = state[0]
            state[0] += 1
            assert place[name] == n, name
            if n >= RING:
                pe.wait_ge(took[reader[n - RING]], count[n - RING])
            return bank[n % RING]

        def chunk(kind, c):
            n = state[1]
            state[1] += 1
            assert chunks[n][:2] == (kind, c)
            pe.wait_ge(wloaded[n % 2], 16 * (n // 2 + 1))
            w = wring[:, n % 2, :]
            return w.rearrange("p (k n) -> p k n", k=KI if kind == "down" else KD)

        def project(w, j, b, src=hT, k=KD):
            for kk in range(k):
                last = mm(b[:, 0:T], w[:, kk, P * j:P * j + P], src[:, kk, :], start=(kk == 0), stop=(kk == k - 1))
            last.then_inc(full, 1)
            return last

        def turns(name, pieces):
            b = opened(name)
            for src, kk, m, col in pieces:
                last = tr(b[0:m, col:col + kk], src, ident[0:kk, 0:kk])
            last.then_inc(full, 1)

        pe.wait_ge(consts, 1)
        pe.wait_ge(ld["rows1"], 64)
        turns("rows1", [(rows1[:, P * c:P * c + P], 34, P, 34 * c) for c in range(KD)])
        pe.wait_ge(ld["rows2"], 64)
        turns("rows2", [(rows2[:, P * c:P * c + P], 7, P, 7 * c) for c in range(KI)])
        pe.wait_ge(ld["histr"], 16)
        for c in range(4):
            turns(("hist", c), [(histr[:, c // 2, P * (4 * (c % 2) + j):P * (4 * (c % 2) + j) + P], 120, P, 120 * j)
                                for j in range(4)])
        pe.wait_ge(ld["mhistr"], 16)
        turns("mhist", [(mhistr[:, P * c:P * c + P], 24, P, 24 * c) for c in range(KI)])
        pe.wait_ge(ld["n0rows"], 16)
        turns("n0", [(n0rows[:, P * c:P * c + P], 32, P, 32 * c) for c in range(HT)])
        for i in range(NT):
            pe.wait_ge(normed, i + 1)
            for c in range(2):
                turns(("hT", i, c), [(h[:, i, P * (4 * c + j):P * (4 * c + j) + P], TT, P, TT * j) for j in range(4)])
        moved(pe, ("hT", 2, 0))
        moved(pe, ("hT", 2, 1))
        for c in range(2):
            for nm, col in (("glu_b", GLU_B), ("glu_a", GLU_A)):
                w = chunk("in", col + 512 * c)
                for j in range(4):
                    project(w, j, opened((nm, 4 * c + j)))
        for c in range(4):
            w = chunk("in", XM + 512 * c)
            for j in range(4):
                project(w, j, opened(("xm", 4 * c + j)))
        for c in range(2):
            w = chunk("in", GA + 512 * c)
            for j in range(4):
                project(w, j, opened(("ga", 4 * c + j)))
        moved(pe, ("glu_a", KD - 1))
        for c in range(2):
            turns(("us", c), [(u[:, 4 * c + j, 0:NS], P, NS, P * j) for j in range(4)])
        for c in range(2):
            turns(("up", c), [(u[:, 4 * c + j, T - CK + 1:T], P, CK - 1, P * j) for j in range(4)])
        moved(pe, ("xm", KI - 1))
        for c in range(4):
            turns(("xs", c), [(xm[:, 4 * c + j, 0:NS], P, NS, P * j) for j in range(4)])
        for c in range(4):
            turns(("xp", c), [(xm[:, 4 * c + j, T - MK + 1:T], P, MK - 1, P * j) for j in range(4)])
        pe.wait_ge(conv_v, 1)
        pe.wait_ge(conv_p, 1)
        for name, src, sig in (("mean", ca, None), ("var", sq, centered)):
            b = opened(name)
            if sig is not None:
                pe.wait_ge(sig, 1)
            for k in range(KD):
                last = mm(b[:, 0:T], ones[:, :], src[:, k, :], start=(k == 0), stop=(k == KD - 1))
            last.then_inc(full, 1)
        pe.wait_ge(conv_act, KD)
        for c in range(2):
            w = chunk("conv_out", 512 * c)
            for j in range(4):
                project(w, j, opened(("ya", 4 * c + j)), src=ca)
        pe.wait_ge(mixed_gates, 1)
        pe.wait_ge(cm_act, KI)
        b = opened("gates")
        for k in range(2 * KI):
            last = mm(b[0:36, 0:T], mif[:, k // KI, k % KI, :], (cm, xm)[k // KI][:, k % KI, :],
                      start=(k == 0), stop=(k == 2 * KI - 1))
        last.then_inc(full, 1)
        pe.wait_ge(se9_set, 1)
        turns("send", [(se9[:, :], NH, 9, 0)])
        pe.wait_ge(exp_out, 3)
        turns("cols", [(st[:, TT * i:TT * i + TT], 68, TT, 68 * i) for i in range(NT)])

        for hd in range(NH):
            b = opened(("bc", hd))
            mm(b[:, 0:T], sel[:, hd, :], nmrow[:, :], start=True, stop=True)
            mm(b[:, T:T + NS], sel[:, hd, :], srow[:, :], start=True, stop=True).then_inc(full, 1)
            pe.wait_ge(wbd_ready, hd + 1)
            for m, nm in enumerate("qk"):
                for c in range(HT):
                    b = opened((nm, hd, c))
                    mm(b[:, 0:T], wbd[:, m, c, :], cm[:, HT * hd + c, :], start=True, stop=True).then_inc(full, 1)
            for m, nm, src in ((1, "kt", cm), (2, "vt", xm)):
                for i in range(NT):
                    b = opened((nm, hd, i))
                    for c in range(HT):
                        last = mm(b[0:TT, P * c:P * c + P], src[:, HT * hd + c, TT * i:TT * i + TT], wbd[:, m, c, :],
                                  start=True, stop=True)
                    last.then_inc(full, 1)
            moved(pe, ("k", hd, HT - 1))
            for i in range(NT):
                b = opened(("s", hd, i))
                for k in range(HT):
                    last = mm(b[0:TT, 0:T], kT[:, k, TT * i:TT * i + TT], qT[:, k, :], start=(k == 0), stop=(k == HT - 1))
                last.then_inc(full, 1)
            moved(pe, ("s", hd, NT - 1))
            pe.wait_ge(qm_ready, hd + 1)
            if hd:
                pe.wait_ge(den_read, hd)
                pe.wait_ge(num0_read, hd)
            for i in range(NT):
                for s in range(i + 1):
                    last = mm(bank[6][0:TT, i:i + 1], pt[:, s, TT * i:TT * i + TT], ones[0:TT, 0:1], start=(s == 0),
                              stop=(s == i))
                if i == 0:
                    for k in range(HT):
                        last = mm(bank[6][0:NS, 0:1], qn[:, k, :], ones[:, 0:1], start=False, stop=(k == HT - 1),
                                  skip_group_check=True)
            last.then_inc(den_full, 1)
            moved(pe, ("vt", hd, NT - 1))
            for i in range(1, NT):
                b = opened(("num", hd, i))
                for s in range(i + 1):
                    last = mm(b[0:TT, :], pt[:, s, TT * i:TT * i + TT], vtok[:, s, :], start=(s == 0), stop=(s == i))
                last.then_inc(full, 1)
            mm(bank[7][0:TT, :], pt[:, 0, 0:TT], vtok[:, 0, :], start=True, stop=True)
            moved(pe, ("kt", hd, NT - 1))
            b = opened(("n1", hd))
            for i in range(NT):
                last = mm(b[0:9, :], wend[:, i, hd, :], ktok[:, i, :], start=(i == 0), stop=(i == NT - 1))
            last.then_inc(full, 1)
            w = chunk("in", OG + 512 * hd)
            for j in range(4):
                project(w, j, opened(("og", hd, j)))
            for s in range(NSEQ):
                e = hd * 9 + s
                c0 = cring[:, e % CR, :, :]
                loads = sum(1 for x in range(e + 1) if x % CR == e % CR and x % 9 < 8)
                pe.wait_ge(c_loaded[e % CR], 16 * loads)
                for k in range(HT):
                    last = mm(bank[7][0:NS, :], qm[:, k, s, :], c0[:, k, :], start=False,
                              stop=(s == NSEQ - 1 and k == HT - 1), skip_group_check=True)
                if s == NSEQ - 1:
                    last.then_inc(num0_full, 1)
                pe.wait_ge(kwm_ready, NSEQ * hd + s + 1)
                for c in range(HT):
                    b = opened(("upd", hd, s, c))
                    mm(b[:, :], kwm[:, s % 2, P * c:P * c + P], vtok[0:NS, 0, :], start=True, stop=True).then_inc(full, 1)
            pe.wait_ge(kend_ready, hd + 1)
            for c in range(HT):
                b = opened(("cp", hd, c))
                for i in range(NT):
                    last = mm(b[:, :], ktok[:, i, P * c:P * c + P], vtok[:, i, :], start=(i == 0), stop=(i == NT - 1))
                last.then_inc(full, 1)
            for i in range(NT):
                pe.wait_ge(hh_ready, NT * hd + (i + 1 if i else NT))
                turns(("hh", hd, i), [(hh[:, i, P * j:P * j + P], TT, P, TT * j) for j in range(4)])
        for c in range(2):
            w = chunk("in", GB + 512 * c)
            for j in range(4):
                project(w, j, opened(("gb", 4 * c + j)))
        pe.wait_ge(hb_ready, NH)
        for c in range(4):
            w = chunk("down", 256 * c)
            for j in range(2):
                project(w, j, opened(("yb", 2 * c + j)), src=cm, k=KI)
        moved(pe, ("yb", KD - 1))
        pe.wait_ge(merged, KD)
        for c in range(2):
            w = chunk("o", 512 * c)
            for i in range(NT):
                b = opened(("op", c, i))
                for k in range(KD):
                    last = mm(b[0:TT, :], yaT[:, k, TT * i:TT * i + TT], w[:, k, :], start=(k == 0), stop=(k == KD - 1))
                last.then_inc(full, 1)
        assert state[0] == len(groups) and state[1] == len(chunks)

    @block.scalar
    def _(act):
        a = nc.scalar
        chain = Signal(sem("act_chain"))
        tk = Signal(took["a"])

        def take(name):
            n = place[name]
            assert reader[n] == "a" and tk.n == count[n] - 1, name
            act.wait_ge(full, n + 1)
            return bank[n % RING]

        for c in range(4):
            b = take(("hist", c))
            tk.inc(a.copy(hist[:, 4 * (c % 2):4 * (c % 2) + 4, 120 * (c // 2):120 * (c // 2) + 120],
                          b[:, 0:480].rearrange("p (c r) -> p c r", c=4)))
        b = take("mhist")
        tk.inc(a.copy(mhist[:, :, :], b[:, 0:384].rearrange("p (c r) -> p c r", c=KI)))
        for i in range(NT):
            b = take(("hT", i, 1))
            tk.inc(a.copy(hT[:, 4:8, TT * i:TT * i + TT], b[:, 0:448].rearrange("p (c r) -> p c r", c=4)))
        for c in range(KD):
            b = take(("glu_b", c))
            if c >= 4:
                moved(act, ("glu_a", c - 4))
            tk.inc(a.activation(sg[:, c % 4, :], b[:, 0:T], ACT.Sigmoid))
        for c in range(KI):
            b = take(("xm", c))
            tk.inc(a.copy(xm[:, c, :], b[:, 0:T]))
        act.wait_ge(normed, NT)
        act.dma_start(ybuf[NE * CAP:YROWS - 3 * CAP, :].rearrange("(r p) n -> p r n", p=CAP),
                      h[0:CAP, 0:1, :].to_broadcast([CAP, MAXO + MAXB, D])).then_inc(filled, 16)
        for c in range(KD):
            b = take(("ga", c))
            tk.inc(a.activation(yaT[:, c, :], b[:, 0:T], ACT.Sigmoid))
        for nm, n, rows, dst in (("us", 2, NS, us_o), ("up", 2, CK - 1, up_o), ("xs", 4, NS, xs_o), ("xp", 4, MK - 1, xp_o)):
            for c in range(n):
                b = take((nm, c))
                tk.inc(a.copy(dst[0:rows, 512 * c:512 * c + 512], b[0:rows, :]))
        act.wait_ge(conv_normed, 1)
        for c in range(KD):
            a.activation(ca[:, c, :], ca[:, c, :], ACT.Silu, bias=cc[:, c, 33:34], scale=cc[:, c, 32:33]).then_inc(conv_act, 1)
        act.wait_ge(mconv_v, 1)
        act.wait_ge(mconv_p, 1)
        for c in range(KI):
            a.activation(cm[:, c, :], cm[:, c, :], ACT.Silu, bias=mc[:, c, 4:5]).then_inc(cm_act, 1)
        act.wait_ge(abs_f, 1)
        step(act, chain, a.activation(gr[:, 3, :], gr[:, 2, :], ACT.Exp, scale=-1.0))
        a.activation(gr[:, 3, :], gr[:, 3, :], ACT.Ln, bias=1.0).then_inc(soft_f, 1)
        act.wait_ge(exp_in, 1)
        a.activation(st[32:36, :], gr[:, 6, :], ACT.Exp, scale=-1.0).then_inc(exp_out, 1)
        a.activation(st[64:68, :], gr[:, 7, :], ACT.Exp).then_inc(exp_out, 1)
        a.activation(srow[:, :], gr[:, 0, 0:NS], ACT.Exp).then_inc(exp_out, 1)
        kw = Signal(kwm_ready)
        for hd in range(NH):
            if hd:
                act.wait_ge(hb_ready, hd)
            else:
                moved(act, "cols")
                act.wait_ge(wends, 1)
                act.wait_ge(stored, 16 * 20)
            for nm, dst in (("q", qT), ("k", kT)):
                for c in range(HT):
                    b = take((nm, hd, c))
                    tk.inc(a.copy(dst[:, c, :], b[:, 0:T]))
            for i in range(NT):
                b = take(("kt", hd, i))
                tk.inc(a.copy(ktok[:, i, :], b[0:TT, :]))
            for i in range(NT):
                act.wait_ge(arg_ready, NT * hd + i + 1)
                a.activation(pt[:, i, :], pt[:, i, :], ACT.Exp, bias=acol[:, i, hd:hd + 1]).then_inc(decay_ready, 1)
            for c in range(HT):
                b = take(("og", hd, c))
                tk.inc(a.activation(kT[:, c, :], b[:, 0:T], ACT.Sigmoid))
            for s in range(NSEQ):
                if s >= 2 or hd:
                    ps, ph = (s - 2, hd) if s >= 2 else (s + NSEQ - 2, hd - 1)
                    computed(act, ("upd", ph, ps, HT - 1))
                if s == 0:
                    moved(act, ("kt", hd, NT - 1))
                kw.inc(a.mul(kwm[:, s % 2, :], ktok[0:NS, 0, :], wend[0:NS, 0, hd, s:s + 1]))
            act.wait_ge(kw.sem, kw.n)
            for i in range(NT):
                step(act, chain, a.mul(ktok[:, i, :], ktok[:, i, :], wend[:, i, hd, 8:9]))
            a.sign(rden[0:1, 3:4], rden[0:1, 3:4]).then_inc(kend_ready, 1)
            e = hd * 9 + NSEQ
            if e >= CR:
                act.wait_ge(c_stored[e % CR], 16 * (e // CR))
            for c in range(HT):
                b = take(("cp", hd, c))
                tk.inc(a.copy(cring[:, e % CR, c, :], b[:, :]))
            act.wait_ge(qm_ready, hd + 1)
            for i in range(NT):
                b = take(("hh", hd, i))
                for j in range(HT):
                    ins = a.mul(qT[:, j, TT * i:TT * i + TT], b[:, TT * j:TT * j + TT], mc[:, HT * hd + j, 6:7])
                    (tk if j == HT - 1 else chain).inc(ins)
        act.wait_ge(hb_ready, NH)
        for c in range(KD):
            b = take(("gb", c))
            tk.inc(a.activation(gb[:, c, :], b[:, 0:T], ACT.Sigmoid))

    @block.vector
    def _(dve):
        v = nc.vector
        chain = Signal(sem("dve_chain"))
        tk = Signal(took["v"])

        def go(ins):
            step(dve, chain, ins)

        def take(name):
            n = place[name]
            assert reader[n] == "v" and tk.n == count[n] - 1, name
            dve.wait_ge(full, n + 1)
            return bank[n % RING]

        b = take("rows1")
        tk.inc(v.tensor_copy(cc[:, :, :], b[:, 0:272].rearrange("p (c r) -> p c r", c=KD)))
        b = take("rows2")
        tk.inc(v.tensor_copy(mc[:, :, :], b[:, 0:112].rearrange("p (c r) -> p c r", c=KI)))
        dve.wait_ge(ld["x0"], 48)
        dve.wait_ge(ld["lnp"], 32)
        nsig = Signal(normed)

        def norm_rows(i, gain, bias, sig):
            x, s = h[:, i, :], lnstat[:, i, :]
            layer_norm_rows(dve, nc, chain, s, x)
            go(v.tensor_tensor(x, x, gain, ALU.mult))
            sig.inc(v.tensor_tensor(x, x, bias, ALU.add))

        norm_rows(0, lng[:, :], lnb[:, :], nsig)
        b = take("n0")
        tk.inc(v.tensor_copy(n0T[:, :, :], b[:, 0:128].rearrange("p (c r) -> p c r", c=HT)))
        for i in range(NT):
            if i < NT - 1:
                dve.wait_ge(ld[f"x{i + 1}"], 16)
                norm_rows(i + 1, lng[:, :], lnb[:, :], nsig)
            b = take(("hT", i, 0))
            tk.inc(v.tensor_copy(hT[:, 0:4, TT * i:TT * i + TT], b[:, 0:448].rearrange("p (c r) -> p c r", c=4)))
        dve.wait_ge(ld["wqkv"], 48)
        dve.wait_ge(ld["wifx"], 16 * 12)
        dve.wait_ge(zeroed, 1)
        for m in range(3):
            for o in range(4):
                dst = mtmp[:, 0 if (o == 0 and m != 1) else 1, :, :]
                go(v.tensor_tensor(dst, wifx[:, m, :, 8 * o:8 * o + 8],
                                   wqkv[:, m, :, o:o + 1].to_broadcast([P, KI, 8]), ALU.mult))
                if o or m == 1:
                    go(v.tensor_tensor(mtmp[:, 0, :, :], mtmp[:, 0, :, :], mtmp[:, 1, :, :], ALU.add))
            if m:
                for j in range(2):
                    go(v.tensor_copy(mif[:, m - 1, :, 32 * j:32 * j + 4], mtmp[:, 0, :, 4 * j:4 * j + 4]))
        v.memset(lnstat[0:1, 0, 0:1], 0.0).then_inc(mixed_gates, 1)
        for c in range(KD):
            b = take(("glu_a", c))
            moved(dve, ("glu_b", c))
            tk.inc(v.tensor_tensor(u[:, c, :], b[:, 0:T], sg[:, c % 4, :], ALU.mult))
        moved(dve, ("hT", 2, 1))
        for c in range(KD):
            moved(dve, ("glu_a", c))
            chain.inc(v.tensor_scalar(ca[:, c, NS:T], u[:, c, NS:T], cc[:, c, CK - 1:CK], cc[:, c, 31:32], ALU.mult, ALU.add))
        for d in range(1, CK):
            for c in range(KD):
                dve.wait_ge(chain.sem, chain.n - KD + 1)
                chain.inc(v.scalar_tensor_tensor(out=ca[:, c, NS + d:T], in0=u[:, c, NS:T - d],
                                                 scalar=cc[:, c, CK - 1 - d:CK - d], in1=ca[:, c, NS + d:T],
                                                 op0=ALU.mult, op1=ALU.add))
        dve.wait_ge(chain.sem, chain.n)
        v.memset(lnstat[0:1, 0, 0:1], 0.0).then_inc(conv_v, 1)
        b = take("mean")
        step(dve, tk, v.tensor_scalar(sg[:, 0, :], b[:, 0:T], 1.0 / D, None, ALU.mult))
        go(v.tensor_tensor(ca[:, :, :], ca[:, :, :], sg[:, 0:1, :].to_broadcast([P, KD, T]), ALU.subtract))
        v.tensor_tensor(sq[:, :, :], ca[:, :, :], ca[:, :, :], ALU.mult).then_inc(centered, 1)
        moved(dve, ("xm", KI - 1))
        for d in range(MK):
            for c in range(KI):
                w = mc[:, c, MK - 1 - d:MK - d]
                if d == 0:
                    chain.inc(v.tensor_scalar(cm[:, c, NS:T], xm[:, c, NS:T], w, None, ALU.mult))
                    continue
                dve.wait_ge(chain.sem, chain.n - KI + 1)
                chain.inc(v.scalar_tensor_tensor(out=cm[:, c, NS + d:T], in0=xm[:, c, NS:T - d], scalar=w,
                                                 in1=cm[:, c, NS + d:T], op0=ALU.mult, op1=ALU.add))
            if d == 0:
                b = take("var")
                step(dve, tk, v.tensor_scalar(sg[:, 0, :], b[:, 0:T], 1.0 / D, None, ALU.mult))
                inverse_root(dve, nc, chain, sg[:, 1, :], sg[:, 0, :], sg[:, 2, :])
                v.tensor_tensor(ca[:, :, :], ca[:, :, :], sg[:, 1:2, :].to_broadcast([P, KD, T]),
                                ALU.mult).then_inc(conv_normed, 1)
        dve.wait_ge(chain.sem, chain.n)
        v.memset(lnstat[0:1, 0, 0:1], 0.0).then_inc(mconv_v, 1)
        for c in range(KD):
            b = take(("ya", c))
            moved(dve, ("ga", c))
            tk.inc(v.tensor_tensor(yaT[:, c, :], b[:, 0:T], yaT[:, c, :], ALU.mult))
        dve.wait_ge(ld["small"], 48)
        dve.wait_ge(consts, N_CONST)
        computed(dve, "gates")
        b = take("gates")
        go(v.tensor_scalar(gr[:, 5, :], b[0:4, 0:T], bif[0:4, :], None, ALU.add))
        step(dve, tk, v.tensor_scalar(gr[:, 1, :], b[32:36, 0:T], bif[32:36, :], None, ALU.add))
        v.scalar_tensor_tensor(out=gr[:, 2, :], in0=gr[:, 1, :], scalar=-1.0, in1=gr[:, 1, :], op0=ALU.mult,
                               op1=ALU.max).then_inc(abs_f, 1)
        go(v.memset(st[:], 0.0))
        go(v.memset(se9[:], 0.0))
        go(v.tensor_scalar(gr[:, 1, :], gr[:, 1, :], 0.0, None, ALU.min))
        dve.wait_ge(soft_f, 1)
        go(v.tensor_tensor(gr[:, 1, :], gr[:, 1, :], gr[:, 3, :], ALU.subtract))
        go(v.tensor_tensor_scan(gr[:, 4, :], segmul[:, :], gr[:, 1, :], 0.0, ALU.mult, ALU.add))
        go(v.tensor_tensor(gr[:, 5, :], gr[:, 5, :], gr[:, 4, :], ALU.subtract))
        go(v.tensor_copy(st[0:4, :], gr[:, 5, :]))
        go(v.tensor_copy(gr[:, 7, :], gr[:, 5, :]))
        s7 = gr[:, 7, 0:NS].rearrange("p (q j) -> p q j", j=LSEQ)
        go(v.tensor_tensor(s7[:, :, 0:1], s7[:, :, 0:1], m0row[:, :].rearrange("p (q a) -> p q a", a=1), ALU.max))
        go(v.tensor_scalar(gr[:, 7, NS:NS + 1], gr[:, 7, NS:NS + 1], 0.0, None, ALU.max))
        go(v.tensor_tensor_scan(gr[:, 3, :], segadd[:, :], gr[:, 7, :], 0.0, ALU.add, ALU.max))
        go(v.tensor_scalar(nmrow[:, :], gr[:, 3, :], -1.0, None, ALU.mult))
        step(dve, Signal(m_ready), v.tensor_tensor(gr[:, 6, :], gr[:, 4, :], gr[:, 3, :], ALU.add))
        M = gr[:, 3, 0:NS].rearrange("p (q j) -> p q j", j=LSEQ)
        a5 = gr[:, 5, 0:NS].rearrange("p (q j) -> p q j", j=LSEQ)
        go(v.tensor_tensor(s7, a5, M[:, :, LSEQ - 1:LSEQ].to_broadcast([NH, NSEQ, LSEQ]), ALU.subtract))
        go(v.tensor_scalar(gr[:, 7, NS:T], gr[:, 5, NS:T], gr[:, 3, T - 1:T], None, ALU.subtract))
        v.tensor_tensor(gr[:, 0, 0:NS].rearrange("p (q j) -> p q j", j=LSEQ),
                        m0row[:, :].rearrange("p (q a) -> p q a", a=1).to_broadcast([NH, NSEQ, LSEQ]), M,
                        ALU.subtract).then_inc(exp_in, 1)
        dve.wait_ge(exp_out, 3)
        v.tensor_copy(se9[:, 0:8].rearrange("p (q a) -> p q a", a=1),
                      srow[:, :].rearrange("p (q j) -> p q j", j=LSEQ)[:, :, LSEQ - 1:LSEQ]).then_inc(se9_set, 1)
        b = take("send")
        step(dve, tk, v.tensor_copy(send9[:, :], b[0:9, 0:4]))
        b = take("cols")
        go(v.memset(wend[:], 0.0))
        step(dve, tk, v.tensor_copy(acol[:, :, :], b[0:TT, 0:NT * 68].rearrange("p (i r) -> p i r", i=NT)))
        go(v.tensor_scalar(acol[:, :, 64:68], acol[:, :, 64:68], SCALE, None, ALU.mult))
        for hd in range(NH):
            go(v.tensor_scalar(wend[0:NS, 0, hd, 0:8], seqmask[:, :], acol[0:NS, 0, 64 + hd:65 + hd], None, ALU.mult))
        go(v.tensor_copy(wend[NS:TT, 0, :, 8], acol[NS:TT, 0, 64:68]))
        go(v.tensor_copy(wend[:, 1, :, 8], acol[:, 1, 64:68]))
        v.tensor_copy(wend[:, 2, :, 8], acol[:, 2, 64:68]).then_inc(wends, 1)
        dve.wait_ge(wends, 1)
        dve.wait_ge(stored, 16 * 20)

        wb, ar, pr, qr, dr, nr, hr, hb = (Signal(s) for s in (wbd_ready, arg_ready, pt_ready, qm_ready, den_read,
                                                              num0_read, hh_ready, hb_ready))
        for hd in range(NH):
            if hd:
                computed(dve, ("hh", hd - 1, NT - 1))
            for m in range(3):
                for c in range(HT):
                    ins = v.tensor_tensor(
                        wbd[:, m, c, :].rearrange("p (b o) -> p b o", o=4),
                        wqkv[:, m, HT * hd + c:HT * hd + c + 1, :].to_broadcast([P, 32, 4]),
                        bmask[:, :].rearrange("p (b o) -> p b o", o=1).to_broadcast([P, 32, 4]), ALU.mult)
                    if m == 2 and c == HT - 1:
                        dve.wait_ge(chain.sem, chain.n)
                        wb.inc(ins)
                    else:
                        chain.inc(ins)
            b = take(("bc", hd))
            go(v.tensor_copy(sbq[:, :], b[:, T:T + NS]))
            for i in range(NT):
                ar.inc(v.tensor_tensor(pt[:, i, :], b[0:TT, 0:T], negmask[:, i, :], ALU.add))
            step(dve, tk, v.tensor_copy(rden[:, 3:4], b[0:TT, 0:1]))
            moved(dve, ("q", hd, HT - 1))
            dve.wait_ge(zeroed, 2)
            for k in range(HT):
                chain.inc(v.tensor_tensor(qs[:, k, :], qT[:, k, 0:NS], sbq[:, :], ALU.mult))
            dve.wait_ge(chain.sem, chain.n)
            for k in range(HT):
                q3 = qs[:, k, :].rearrange("p (q j) -> p q j", j=LSEQ)
                diag = bass.AP(qm[:, k, :, :].tensor, qm[:, k, :, :].offset, [list(x) for x in qm[:, k, :, :].ap][:1] + [[NS + LSEQ, NSEQ], [1, LSEQ]])
                chain.inc(v.tensor_copy(diag, q3))
                n3 = n0T[:, k, :].rearrange("p (q g) -> p q g", g=NH)[:, :, hd:hd + 1].to_broadcast([P, NSEQ, LSEQ])
                chain.inc(v.tensor_tensor(qn[:, k, :].rearrange("p (q j) -> p q j", j=LSEQ), q3, n3, ALU.mult))
            dve.wait_ge(chain.sem, chain.n)
            qr.inc(v.tensor_copy(rden[0:1, 3:4], rden[0:1, 3:4]))
            for i in range(NT):
                b = take(("vt", hd, i))
                tk.inc(v.tensor_copy(vtok[:, i, :], b[0:TT, :]))
            for i in range(NT):
                b = take(("s", hd, i))
                dve.wait_ge(decay_ready, NT * hd + i + 1)
                tk.inc(v.scalar_tensor_tensor(out=pt[:, i, :], in0=b[0:TT, 0:T], scalar=SCALE, in1=pt[:, i, :],
                                              op0=ALU.mult, op1=ALU.mult))
            dve.wait_ge(den_full, hd + 1)
            step(dve, dr, v.tensor_copy(rden[:, 0:NT], bank[6][0:TT, 0:NT]))
            go(v.scalar_tensor_tensor(out=rden[:, 0:NT], in0=rden[:, 0:NT], scalar=-1.0, in1=rden[:, 0:NT],
                                      op0=ALU.mult, op1=ALU.max))
            go(v.tensor_tensor(rden[:, 0:NT], rden[:, 0:NT], acol[:, :, 32 + hd], ALU.max))
            go(v.reciprocal(rden[:, 0:NT], rden[:, 0:NT]))

            def finish(i, b, read):
                x, s = hh[:, i, :], lnstat[:, i, :]
                step(dve, read, v.tensor_scalar(x, b[0:TT, :], rden[:, i:i + 1], None, ALU.mult))
                go(v.bn_stats(s[:, 0:6], x))
                go(v.bn_aggr(s[:, 12:14], s[:, 0:6]))
                inverse_root(dve, nc, chain, s[:, 14:15], s[:, 13:14], s[:, 15:16])
                hr.inc(v.tensor_scalar(x, x, s[:, 12:13], s[:, 14:15], ALU.subtract, ALU.mult))

            for i in range(1, NT):
                finish(i, take(("num", hd, i)), tk)
            b = take(("n1", hd))
            dve.wait_ge(n0_loaded, 16 * (hd + 1))
            if hd:
                dve.wait_ge(n1_stored, 32 * hd)
            tk.inc(v.scalar_tensor_tensor(out=n1o[:, :], in0=n0x[:, :], scalar=send9[:, hd:hd + 1], in1=b[0:9, :],
                                          op0=ALU.mult, op1=ALU.add))
            for s in range(NSEQ):
                e = hd * 9 + s
                for c in range(HT):
                    b = take(("upd", hd, s, c))
                    cv = cring[:, e % CR, c, :]
                    tk.inc(v.scalar_tensor_tensor(out=cv, in0=cv, scalar=sbq[:, LSEQ * s + LSEQ - 1:LSEQ * s + LSEQ],
                                                  in1=b[:, :], op0=ALU.mult, op1=ALU.add))
            dve.wait_ge(num0_full, hd + 1)
            finish(0, bank[7], nr)
            moved(dve, ("hh", hd, NT - 1))
            moved(dve, ("og", hd, HT - 1))
            for c in range(HT):
                x = cm[:, HT * hd + c, :]
                go(v.scalar_tensor_tensor(out=x, in0=x, scalar=mc[:, HT * hd + c, 5:6], in1=qT[:, c, :],
                                          op0=ALU.mult, op1=ALU.add))
                ins = v.tensor_tensor(x, x, kT[:, c, :], ALU.mult)
                if c == HT - 1:
                    dve.wait_ge(chain.sem, chain.n)
                    hb.inc(ins)
                else:
                    chain.inc(ins)
        mg = Signal(merged)
        for c in range(KD):
            b = take(("yb", c))
            moved(dve, ("gb", c))
            step(dve, tk, v.tensor_tensor(gb[:, c, :], b[:, 0:T], gb[:, c, :], ALU.mult))
            mg.inc(v.tensor_tensor(yaT[:, c, :], yaT[:, c, :], gb[:, c, :], ALU.add))
        dve.wait_ge(filled, 16)
        for c in range(2):
            for i in range(NT):
                b = take(("op", c, i))
                x = h[:, i, 512 * c:512 * c + 512]
                tk.inc(v.scalar_tensor_tensor(out=x, in0=x, scalar=ALPHA, in1=b[0:TT, :], op0=ALU.mult, op1=ALU.add))
        dve.wait_ge(tk.sem, tk.n)
        dve.wait_ge(ld["ln1"], 32)
        es = Signal(embedded)
        for i in range(NT):
            norm_rows(i, ln1g[:, :], ln1b[:, :], es)
        assert tk.n == reader.count("v")


def moe(nc, ctx, part, sb, bank, I, O, ybuf, h, hT, ident, ones, lnstat):
    def sem(name):
        return ctx.enter_context(nc.semaphore(name))

    end = sb.end
    WS = 4
    wx = [[sb(f"w1_{s}", [P, KD, FE]), sb(f"w3_{s}", [P, KD, FE]), sb(f"w2_{s}", [P, 2, D])] for s in range(WS)]
    gbuf = [sb(f"gbuf{i}", [TT, D], at=end["w1_0"] - 8192 + 4096 * i) for i in range(NG_BUF)]
    lg = sb("lg", [TT, D], at=end["w1_2"])
    lb = sb("lb", [TT, D], at=end["lg"])
    acc = sb("acc", [TT, NT, D])
    hb = sb("hb", [TT, NT, 3, KD, P], dt=BF16)
    hr = sb("hr", [TT, D])
    wr = sb("wr", [P, KD, NE])
    rbias = sb("rbias", [TT, NE])
    sc = sb("sc", [TT, NT, NE])
    ch = sb("ch", [TT, NT, NE])
    wt = sb("wt", [TT, NT, NE])
    mask = sb("mask", [TT, NT, NE])
    rank = sb("rank", [TT, NT, NE + 1])
    key = sb("key", [TT, NT, NE])
    rt = sb("rt", [TT, 5, NE])
    kv = sb("kv", [TT, NT, TOP_K])
    idx = sb("idx", [TT, NT, TOP_K], dt=I32)
    w8 = sb("w8", [TT, NT, TOP_K])
    t8 = sb("t8", [TT, NG, 8])
    gs = sb("gs", [TT, 4, 8])
    rs = sb("rs", [TT, 2])
    tab = sb("tab", [1, 3, NE], dt=I32)
    before = sb("before", [TT, TT])
    slot = sb("slot", [TT, CAP * (MAXB + 1)])
    ecol = sb("ecol", [TT, NE])
    silu = sb("silu", [P, 2, T])
    act_ = sb("act_", [P, 2, T])
    xg = sb("xg", [P, 2, KD, CAP])
    S = sb("S", [TT, 3, NT, CAP], dt=BF16)
    sgu = sb("sgu", [CAP, 2, FE])
    hm = sb("hm", [CAP, 2, FE])
    hmT = sb("hmT", [P, 2, 2, CAP])
    ys = sb("ys", [P, 3, 512])

    XB, GUB, TB, YB = bank[0:2], bank[2:4], bank[4], bank[5:7]
    loaded = [sem(f"e_loaded{i}") for i in range(WS)]
    parm, lnp, turned, hT_set, hT_a = sem("moe_parm"), sem("lnp2"), sem("turned"), sem("hT_set"), sem("hT_a")
    mconst = sem("moe_consts")
    logits, scored, ranked, split, masked, tabled = (
        sem(n) for n in ("logits", "scored", "ranked", "split", "masked", "tabled"))
    sh_gu, sh_silu, sh_act, sh_out, sh_took = (sem(n) for n in ("sh_gu", "sh_silu", "sh_act", "sh_out", "sh_took"))
    sh_loaded = sem("sh_loaded")
    names = ("onehot", "x_full", "x_set", "gu_full", "silued", "gated", "t_full", "t_set", "y_full", "y_set")
    m = {n: sem("m_" + n) for n in names}
    o = {n: sem("o_" + n) for n in names}
    y_stored = [sem("y_stored0"), sem("y_stored1")]
    o_stored = sem("o_stored")
    fetched = [sem(f"fetched{i}") for i in range(NG_BUF)]
    used = sem("used")
    normed2, out_stored = sem("normed2"), sem("out_stored")
    block = part.enter_context(nc.Block())
    srcs = (I["w_e1"][0], I["w_e3"][0], I["w_e2"][0])
    shared = (I["w_s1"][0], I["w_s3"][0], I["w_s2"][0])
    OROW = NE * CAP

    def load(sp, sig, w, srcs3):
        for dst, src in zip(w, srcs3):
            sp.dma_start(dst[:, :, :], src.rearrange("(p k) n -> p k n", p=P)).then_inc(sig, 16)

    def counts(eng, r):
        _, vals = nc.values_load_multi_w_load_instructions(
            tab[0:1, 0, bass.ds(r * WS, WS)], engines=[eng.engine], min_val=0, max_val=MAXB - 1,
            skip_runtime_bounds_check_because="at most T tokens go to an expert")
        return vals

    def further(eng, e, n, body):
        with eng.If(n > 0):
            first = eng.value_load(tab[0:1, 1, bass.ds(e, 1)], min_val=0, max_val=MAXO)
            with eng.Fori(0, n) as b:
                body(b, first + b)
            eng.nop()

    @block.sync
    def _(sp):
        load(sp, sh_loaded, wx[WS - 1], shared)
        sp.dma_start(wr[:, :, :], I["w_router"][0].rearrange("(p k) n -> p k n", p=P)).then_inc(parm, 16)
        sp.dma_start(rbias[:, :], I["router_bias"].to_broadcast([TT, NE])).then_inc(parm, 16)
        for e in range(WS):
            if e == WS - 1:
                sp.wait_ge(sh_out, 6)
            load(sp, loaded[e], wx[e], [w[e] for w in srcs])
        with sp.Fori(1, NE // WS) as r:
            for j in range(WS):
                e = r * WS + j
                sp.wait_ge(m["gu_full"], r * WS + (j - WS + 2))
                load(sp, loaded[j], wx[j], [w[e] for w in srcs])
        sp.wait_ge(m["y_full"], NE)
        sp.wait_ge(tabled, 2)
        sp.dma_start(lg[:, :], I["ln2_g"].to_broadcast([TT, D])).then_inc(lnp, 16)
        sp.dma_start(lb[:, :], I["ln2_b"].to_broadcast([TT, D])).then_inc(lnp, 16)

    @block.gpsimd
    def _(pool):
        g = nc.gpsimd
        chain = Signal(sem("moe_pool"))
        step(pool, chain, g.memset(before[:], 1.0))
        g.affine_select(out=before[:, :], in_=before[:, :], compare_op=ALU.is_gt, fill=0.0, base=0,
                        pattern=[[1, TT]], channel_multiplier=-1).then_inc(mconst, 1)
        g.iota(slot[:, :], pattern=[[1, CAP * (MAXB + 1)]], base=0, channel_multiplier=0,
               allow_small_or_imprecise_dtypes=True).then_inc(mconst, 1)
        g.iota(ecol[:, :], pattern=[[CAP, NE]], base=0, channel_multiplier=0,
               allow_small_or_imprecise_dtypes=True).then_inc(mconst, 1)
        step(pool, chain, g.memset(ys[:], 0.0))

        def store(src, row, sig):
            pool.wait_ge(mconst, 3)
            for c in range(2):
                pool.dma_start(ybuf[bass.ds(row, CAP), 512 * c:512 * c + 512], ys[CAP * c:CAP * c + CAP, src, :]
                               ).then_inc(sig, 16)

        for src, sig in ((0, y_stored[0]), (1, y_stored[1]), (2, o_stored)):
            store(src, YROWS - CAP * (3 - src), sig)
        pool.wait_ge(tabled, 1)
        with pool.Fori(0, NE // WS) as r:
            ns = counts(pool, r)
            for j in range(WS):
                e = r * WS + j
                pool.wait_ge(m["y_set"], r * WS + (j + 3))
                store(j % 2, r * (WS * CAP) + j * CAP, y_stored[j % 2])

                def body(b, n):
                    pool.wait_ge(o["y_set"], n + 1)
                    store(2, n * CAP + OROW, o_stored)

                further(pool, e, ns[j], body)
        for s in range(2):
            pool.wait_ge(y_stored[s], 32 * (NE // 2 + 1))
        total = pool.value_load(tab[0:1, 2, 0:1], min_val=0, max_val=MAXO)
        pool.wait_ge(o_stored, total * 32 + 32)
        step(pool, chain, g.tensor_tensor(ecol[:, 0:1], ecol[:, 0:1], ecol[:, 0:1], ALU.mult))
        for n in range(NT * TOP_K):
            i, k = n // TOP_K, n % TOP_K
            if n >= NG_BUF:
                pool.wait_ge(used, n - NG_BUF + 1)
            pool.indirect_dma_start(out=gbuf[n % NG_BUF][:, :], out_offset=None, in_=ybuf[:, :],
                                    in_offset=bass.IndirectOffsetOnAxis(ap=idx[:, i, k:k + 1], axis=0),
                                    bounds_check=YROWS - 1).then_inc(fetched[n % NG_BUF], 16)

    @block.tensor
    def _(pe):
        mm, tr = nc.tensor.matmul, nc.tensor.transpose
        tn = Signal(turned)
        for i in range(NT):
            for c in range(2):
                for j in range(4):
                    last = tr(bank[2 * i + c][:, TT * j:TT * j + TT], h[:, i, 4 * c + j:D:KD], ident[0:TT, 0:TT])
                tn.inc(last)
        pe.wait_ge(hT_set, 3)
        pe.wait_ge(hT_a, 3)
        pe.wait_ge(parm, 32)
        for i in range(NT):
            for k in range(KD):
                last = mm(bank[7][0:TT, NE * i:NE * i + NE], hT[:, k, TT * i:TT * i + TT], wr[:, k, :],
                          start=(k == 0), stop=(k == KD - 1))
        last.then_inc(logits, 1)
        pe.wait_ge(sh_loaded, 48)
        w1, w3, w2 = wx[WS - 1]
        for j in range(2):
            for w, b in ((w1, bank[j]), (w3, bank[2 + j])):
                for k in range(KD):
                    last = mm(b[:, 0:T], w[:, k, j:FE:2], hT[:, k, :], start=(k == 0), stop=(k == KD - 1))
                last.then_inc(sh_gu, 1)
        pe.wait_ge(sh_act, 2)
        for x in range(6):
            i, c = x // 2, x % 2
            if x >= 3:
                pe.wait_ge(sh_took, x - 2)
            for j in range(2):
                last = mm(bank[4 + x % 3][0:TT, :], act_[:, j, TT * i:TT * i + TT], w2[:, j, 512 * c:512 * c + 512],
                          start=(j == 0), stop=(j == 1))
            last.then_inc(sh_out, 1)
        pe.wait_ge(mconst, 3)
        pe.wait_ge(masked, 1)
        for i in range(NT):
            for s in range(i + 1):
                mm(bank[7][0:TT, NE * i:NE * i + NE], before[:, :] if s == i else ones[0:TT, 0:TT], mask[:, s, :],
                   start=(s == 0), stop=(s == i))
        for s in range(NT):
            last = mm(bank[7][0:TT, NE * NT:NE * NT + NE], ones[0:TT, 0:TT], mask[:, s, :], start=(s == 0),
                      stop=(s == NT - 1))
        last.then_inc(ranked, 1)

        def gather(s, hot, sig):
            for k in range(KD):
                for i in range(NT):
                    for p in range(3):
                        last = mm(XB[s][:, CAP * k:CAP * k + CAP], hb[:, i, p, k, :], S[:, hot, i, :],
                                  start=(i == 0 and p == 0), stop=(i == NT - 1 and p == 2))
            last.then_inc(sig["x_full"], 1)

        def gate_up(s, w, sig):
            for k in range(KD):
                for half in range(2):
                    last = mm(GUB[s][CAP * half:CAP * half + CAP, 0:FE], xg[:, s, k, :], wx[w][half][:, k, :],
                              start=(k == 0), stop=(k == KD - 1))
            last.then_inc(sig["gu_full"], 1)

        def turn(s, sig):
            for j in range(2):
                last = mm(TB[:, CAP * j:CAP * j + CAP], hm[:, s, j:FE:2], ident[0:CAP, 0:CAP], start=True, stop=True)
            last.then_inc(sig["t_full"], 1)

        def down(s, w, sig):
            for j in range(2):
                for c in range(2):
                    last = mm(YB[s][CAP * c:CAP * c + CAP, :], hmT[:, s, j, :], wx[w][2][:, j, 512 * c:512 * c + 512],
                              start=(j == 0), stop=(j == 1))
            last.then_inc(sig["y_full"], 1)

        pe.wait_ge(split, NT)
        pe.wait_ge(m["onehot"], 1)
        pe.wait_ge(sh_took, 6)
        gather(0, 0, m)
        pe.wait_ge(tabled, 1)
        with pe.Fori(0, NE // WS) as r:
            ns = counts(pe, r)
            for j in range(WS):
                s, base = j % 2, r * WS
                pe.wait_ge(loaded[j], r * 48 + 48)
                pe.wait_ge(m["x_set"], base + (j + 2))
                gate_up(s, j, m)
                pe.wait_ge(m["onehot"], base + (j + 2))
                gather(1 - s, 1 - s, m)
                pe.wait_ge(m["gated"], base + (j + 1))
                turn(s, m)
                pe.wait_ge(m["t_set"], base + (j + 1))
                pe.wait_ge(m["y_set"], base + (j + 1))
                down(s, j, m)

                def body(b, n):
                    pe.wait_ge(o["onehot"], n + 1)
                    gather(s, 2, o)
                    pe.wait_ge(o["x_set"], n + 1)
                    gate_up(s, j, o)
                    pe.wait_ge(o["gated"], n + 1)
                    turn(s, o)
                    pe.wait_ge(o["t_set"], n + 1)
                    pe.wait_ge(m["y_set"], base + (j + 3))
                    down(s, j, o)
                    pe.wait_ge(o["y_set"], n + 1)

                further(pe, base + j, ns[j], body)

    @block.scalar
    def _(act):
        a = nc.scalar
        for i in range(NT):
            act.wait_ge(turned, 2 * i + 2)
            a.copy(hT[:, 4:8, TT * i:TT * i + TT],
                   bank[2 * i + 1][:, 0:448].rearrange("p (c r) -> p c r", c=4)).then_inc(hT_a, 1)
        act.wait_ge(logits, 1)
        a.activation(sc[:, :, :], bank[7][0:TT, 0:NT * NE].rearrange("p (i e) -> p i e", i=NT),
                     ACT.Sigmoid).then_inc(scored, 1)
        for j in range(2):
            act.wait_ge(sh_gu, 2 * j + 1)
            a.activation(silu[:, j, :], bank[j][:, 0:T], ACT.Silu).then_inc(sh_silu, 1)
        for x in range(6):
            act.wait_ge(sh_out, x + 1)
            a.copy(acc[:, x // 2, 512 * (x % 2):512 * (x % 2) + 512], bank[4 + x % 3][0:TT, :]).then_inc(sh_took, 1)

        def copy_x(s, sig):
            a.copy(xg[:, s, :, :], XB[s][:, :].rearrange("p (k c) -> p k c", c=CAP)).then_inc(sig["x_set"], 1)

        def gate(s, sig):
            a.activation(sgu[:, s, :], GUB[s][0:CAP, 0:FE], ACT.Silu).then_inc(sig["silued"], 1)

        a.copy(silu[0:1, 0, 0:1], ident[0:1, 0:1]).then_inc(m["x_set"], 1)
        act.wait_ge(m["x_full"], 1)
        copy_x(0, m)
        act.wait_ge(tabled, 1)
        with act.Fori(0, NE // WS) as r:
            ns = counts(act, r)
            for j in range(WS):
                s, base = j % 2, r * WS
                act.wait_ge(m["gu_full"], base + (j + 1))
                gate(s, m)
                act.wait_ge(m["x_full"], base + (j + 2))
                copy_x(1 - s, m)

                def body(b, n):
                    act.wait_ge(o["x_full"], n + 1)
                    copy_x(s, o)
                    act.wait_ge(o["gu_full"], n + 1)
                    gate(s, o)

                further(act, base + j, ns[j], body)
        for i in range(NT):
            act.wait_ge(normed2, i + 1)
            if i == 0:
                act.dma_start(O["y_sample"].rearrange("b l d -> (b l) d"), h[0:NS, 0, :]).then_inc(out_stored, 16)
                act.dma_start(O["y_prompt"][0, 0:32, :], h[80:112, 0, :]).then_inc(out_stored, 16)
            else:
                act.dma_start(O["y_prompt"][0, TT * i - 80:TT * i + 32, :], h[:, i, :]).then_inc(out_stored, 16)
        act.wait_ge(out_stored, 64)

    @block.vector
    def _(dve):
        v = nc.vector
        chain = Signal(sem("moe_chain"))

        def go(ins):
            step(dve, chain, ins)

        for i in range(NT):
            dve.wait_ge(turned, 2 * i + 1)
            v.tensor_copy(hT[:, 0:4, TT * i:TT * i + TT],
                          bank[2 * i][:, 0:448].rearrange("p (c r) -> p c r", c=4)).then_inc(hT_set, 1)
        sp_ = Signal(split)
        for i in range(NT):
            def parts(x):
                return x.rearrange("t (p k) -> t k p", k=KD)

            go(v.tensor_copy(hb[:, i, 0, :, :], parts(h[:, i, :])))
            go(v.tensor_tensor(hr[:, :].rearrange("t (k p) -> t k p", k=KD), parts(h[:, i, :]), hb[:, i, 0, :, :],
                               ALU.subtract))
            go(v.tensor_copy(hb[:, i, 1, :, :], hr[:, :].rearrange("t (k p) -> t k p", k=KD)))
            step(dve, sp_, v.tensor_tensor(hb[:, i, 2, :, :], hr[:, :].rearrange("t (k p) -> t k p", k=KD),
                                           hb[:, i, 1, :, :], ALU.subtract))
        dve.wait_ge(scored, 1)
        dve.wait_ge(parm, 32)

        def route(i):
            s, c, w = sc[:, i, :], ch[:, i, :], wt[:, i, :]
            go(v.tensor_tensor(c, s, rbias[:, :], ALU.add))
            for g in range(NG):
                chain.inc(v.max(t8[:, g, :], c[:, GE * g:GE * g + GE]))
            dve.wait_ge(chain.sem, chain.n)
            go(v.tensor_tensor(gs[:, 0, :], t8[:, :, 0], t8[:, :, 1], ALU.add))
            go(v.max(gs[:, 1, :], gs[:, 0, :]))
            go(v.memset(gs[:, 1, 4:8], -NEG))
            go(v.match_replace(gs[:, 2, :], gs[:, 1, :], gs[:, 0, :], NEG))
            go(v.tensor_tensor(gs[:, 3, :], gs[:, 0, :], gs[:, 2, :], ALU.is_equal))
            go(v.tensor_scalar(gs[:, 3, :], gs[:, 3, :], NEG, None, ALU.mult))
            go(v.tensor_tensor(c.rearrange("p (g e) -> p g e", e=GE), c.rearrange("p (g e) -> p g e", e=GE),
                               gs[:, 3, :].rearrange("p (g a) -> p g a", a=1).to_broadcast([TT, NG, GE]), ALU.add))
            go(v.max(t8[:, 0, :], c))
            go(v.match_replace(w, t8[:, 0, :], c, 2 * NEG))
            go(v.tensor_tensor(mask[:, i, :], c, w, ALU.not_equal))
            go(v.tensor_tensor(w, mask[:, i, :], s, ALU.mult))
            go(v.tensor_reduce(rs[:, 0:1], w, AX.X, ALU.add))
            go(v.reciprocal(rs[:, 1:2], rs[:, 0:1]))
            go(v.tensor_scalar(w, w, rs[:, 1:2], ROUTE_SCALE, ALU.mult, ALU.mult))

        for i in range(NT):
            route(i)
            if i < 2:
                dve.wait_ge(sh_silu, i + 1)
                dve.wait_ge(sh_gu, 2 * i + 2)
                v.tensor_tensor(act_[:, i, :], silu[:, i, :], bank[2 + i][:, 0:T], ALU.mult).then_inc(sh_act, 1)
        v.memset(rank[:], -1.0).then_inc(masked, 1)
        dve.wait_ge(masked, 1)
        dve.wait_ge(ranked, 1)
        dve.wait_ge(mconst, 3)
        go(v.tensor_copy(rt[:, 0, :], bank[7][0:TT, NE * NT:NE * NT + NE]))
        go(v.tensor_scalar(rt[:, 1, :], rt[:, 0, :], float(CAP), None, ALU.is_gt))
        for b in range(2, MAXB):
            go(v.scalar_tensor_tensor(out=rt[:, 1, :], in0=rt[:, 0, :], scalar=float(CAP * b), in1=rt[:, 1, :],
                                      op0=ALU.is_gt, op1=ALU.add))
        go(v.tensor_tensor_scan(rt[:, 2, :], ones[0:TT, 0:NE], rt[:, 1, :], 0.0, ALU.mult, ALU.add))
        go(v.tensor_tensor(rt[:, 3, :], rt[:, 2, :], rt[:, 1, :], ALU.subtract))
        go(v.tensor_copy(tab[:, 0, :], rt[0:1, 1, :]))
        go(v.tensor_copy(tab[:, 1, :], rt[0:1, 3, :]))
        step(dve, Signal(tabled), v.tensor_copy(tab[:, 2, 0:1], rt[0:1, 2, NE - 1:NE]))
        for i in range(NT):
            rk = bank[7][0:TT, NE * i:NE * i + NE]
            go(v.tensor_scalar(rt[:, 0, :], rk, 1.0, None, ALU.add))
            go(v.tensor_tensor(rt[:, 0, :], rt[:, 0, :], mask[:, i, :], ALU.mult))
            go(v.tensor_scalar(rank[:, i, 0:NE], rt[:, 0, :], -1.0, None, ALU.add))

        def one_hot(i, hot, e, first):
            return v.tensor_scalar(S[:, hot, i, :], slot[:, bass.ds(first, CAP)], rank[:, i, bass.ds(e, 1)], None,
                                   ALU.is_equal)

        def hots(hot, e, first, sig):
            for i in range(NT):
                ins = one_hot(i, hot, e, first)
                if i == NT - 1:
                    ins.then_inc(sig["onehot"], 1)
                else:
                    chain.inc(ins)

        hots(0, 0, 0, m)
        go(v.tensor_scalar(rt[:, 3, :], rt[:, 3, :], float(CAP), float(OROW - CAP), ALU.mult, ALU.add))
        go(v.tensor_tensor(rt[:, 3, :], rt[:, 3, :], ecol[:, :], ALU.subtract))
        for i in range(NT):
            go(v.scalar_tensor_tensor(out=rt[:, 4, :], in0=rank[:, i, 0:NE], scalar=float(CAP), in1=rt[:, 3, :],
                                      op0=ALU.is_ge, op1=ALU.mult))
            go(v.tensor_tensor(rt[:, 4, :], rt[:, 4, :], rank[:, i, 0:NE], ALU.add))
            go(v.tensor_tensor(rt[:, 4, :], rt[:, 4, :], ecol[:, :], ALU.add))
            go(v.scalar_tensor_tensor(out=key[:, i, :], in0=rt[:, 4, :], scalar=1.0, in1=mask[:, i, :], op0=ALU.add,
                                      op1=ALU.mult))
            go(v.max(kv[:, i, :], key[:, i, :]))
            for k in range(TOP_K):
                go(v.scalar_tensor_tensor(out=rt[:, 0, :], in0=key[:, i, :], scalar=kv[:, i, k:k + 1],
                                          in1=wt[:, i, :], op0=ALU.is_equal, op1=ALU.mult))
                go(v.tensor_reduce(w8[:, i, k:k + 1], rt[:, 0, :], AX.X, ALU.add))
            go(v.tensor_scalar(kv[:, i, :], kv[:, i, :], -1.0, None, ALU.add))
            go(v.tensor_copy(idx[:, i, :], kv[:, i, :]))
        for _ in range(2):
            step(dve, chain, v.memset(rt[0:1, 0, 0:1], 0.0))
            v.memset(rt[0:1, 0, 1:2], 0.0).then_inc(m["y_set"], 1)

        def gate(s, sig):
            v.tensor_tensor(hm[:, s, :], sgu[:, s, :], GUB[s][CAP:P, 0:FE], ALU.mult).then_inc(sig["gated"], 1)

        def copy_t(s, sig):
            v.tensor_copy(hmT[:, s, :, :], TB[:, 0:2 * CAP].rearrange("p (j c) -> p j c", j=2)).then_inc(sig["t_set"], 1)

        with dve.Fori(0, NE // WS) as r:
            ns = counts(dve, r)
            for j in range(WS):
                s, base = j % 2, r * WS
                dve.wait_ge(m["x_full"], base + (j + 1))
                for i in range(NT):
                    ins = one_hot(i, 1 - s, base + (j + 1), 0)
                ins.then_inc(m["onehot"], 1)
                dve.wait_ge(m["silued"], base + (j + 1))
                gate(s, m)
                dve.wait_ge(m["t_full"], base + (j + 1))
                copy_t(s, m)
                dve.wait_ge(m["y_full"], base + (j + 1))
                dve.wait_ge(y_stored[s], r * 64 + (32 * (j // 2) + 32))
                v.tensor_copy(ys[:, s, :], YB[s][:, :]).then_inc(m["y_set"], 1)

                def body(b, n):
                    for i in range(NT):
                        ins = one_hot(i, 2, base + j, b * CAP + CAP)
                    ins.then_inc(o["onehot"], 1)
                    dve.wait_ge(o["silued"], n + 1)
                    gate(s, o)
                    dve.wait_ge(o["t_full"], n + 1)
                    copy_t(s, o)
                    dve.wait_ge(o["y_full"], n + 1)
                    dve.wait_ge(o_stored, n * 32 + 32)
                    v.tensor_copy(ys[:, 2, :], YB[s][:, :]).then_inc(o["y_set"], 1)

                further(dve, base + j, ns[j], body)
        v.memset(rt[0:1, 0, 0:1], 0.0).then_inc(tabled, 1)
        for n in range(NT * TOP_K):
            i, k = n // TOP_K, n % TOP_K
            dve.wait_ge(fetched[n % NG_BUF], 16 * (n // NG_BUF + 1))
            if k:
                dve.wait_ge(used, n)
            v.scalar_tensor_tensor(out=acc[:, i, :], in0=gbuf[n % NG_BUF][:, :], scalar=w8[:, i, k:k + 1],
                                   in1=acc[:, i, :], op0=ALU.mult, op1=ALU.add).then_inc(used, 1)
        dve.wait_ge(used, NT * TOP_K)
        dve.wait_ge(lnp, 32)
        nsig = Signal(normed2)
        for i in range(NT):
            x = h[:, i, :]
            go(v.scalar_tensor_tensor(out=x, in0=x, scalar=ALPHA, in1=acc[:, i, :], op0=ALU.mult, op1=ALU.add))
            layer_norm_rows(dve, nc, chain, lnstat[:, i, :], x)
            go(v.tensor_tensor(x, x, lg[:, :], ALU.mult))
            nsig.inc(v.tensor_tensor(x, x, lb[:, :], ALU.add))


_INS = ["x_prompt", "x_sample", "state_conv", "state_mconv", "state_C", "state_n", "state_m", "meta_tokens",
        "ln_in_g", "ln_in_b", "w_in", "conv_w", "conv_b", "conv_ln_g", "conv_ln_b", "w_conv_out", "mconv_w", "mconv_b",
        "w_q", "w_k", "w_v", "w_if", "b_if", "mh_ln_g", "skip", "w_m_down", "w_o", "ln1_g", "ln1_b", "ln2_g", "ln2_b",
        "w_router", "router_bias", "w_e1", "w_e3", "w_e2", "w_s1", "w_s3", "w_s2"]
_OUTS = {"y_prompt": (1, SEQ, D), "y_sample": (NSEQ, LSEQ, D), "conv_p": (1, 1, CK - 1, D),
         "mconv_p": (1, 1, MK - 1, DI), "C_p": (1, 1, NH, HD, HD), "n_p": (1, 1, NH, HD), "m_p": (1, 1, NH),
         "conv_s": (1, NSEQ, CK - 1, D), "mconv_s": (1, NSEQ, MK - 1, DI), "C_s": (1, NSEQ, NH, HD, HD),
         "n_s": (1, NSEQ, NH, HD), "m_s": (1, NSEQ, NH)}


def kernel(**inputs):
    import numpy as _np
    import concourse.bacc as _bacc
    from concourse import mybir as _mybir
    from concourse.bass_utils import run_bass_kernel_spmd as _run

    nc = _bacc.Bacc("TRN2", target_bir_lowering=False, num_devices=1)
    arrays, I, O = {}, {}, {}
    for name in _INS:
        a = _np.ascontiguousarray(inputs[name])
        arrays[f"in_{name}"] = a
        I[name] = nc.dram_tensor(f"in_{name}", a.shape, _mybir.dt.from_np(a.dtype), kind="ExternalInput").ap()
    for name, shape in _OUTS.items():
        O[name] = nc.dram_tensor(f"out_{name}", shape, _mybir.dt.float32, kind="ExternalOutput").ap()
    build(nc, I, O)
    r = _run(nc, [arrays], core_ids=[0])
    return tuple(r.results[0][f"out_{name}"] for name in _OUTS)
```
